# Optimizing a Trainium2 kernel written in Bass

```python
import math
import jax, jax.numpy as jnp
from jax import lax
import numpy as np

D_MODEL = 1024
BATCH = 1
SEQ = 128
DEPTH = 2
DEC_BATCH = 1
DEC_SEQ = 512
PAST_LEN = 128

GRID_W = 64
D_MIX = 1024
EPS = 1e-6
MLA_HEADS = 4
Q_LORA = 256
KV_LORA = 128
QK_NOPE = 64
QK_ROPE = 32
V_HEAD = 64
MLA_OUT = MLA_HEADS * V_HEAD
ROPE_THETA = 10000.0
ROPE_FREQS = QK_ROPE // 4
MLA_SCALE = (QK_NOPE + QK_ROPE) ** -0.5
ATTN_BLOCK = 128
SSD_HEADS = 8
SSD_HEADDIM = 64
SSD_INNER = SSD_HEADS * SSD_HEADDIM
SSD_GROUPS = 2
SSD_DSTATE = 64
SSD_CONV = 5
SSD_CHUNK = 128
SSD_CONV_DIM = SSD_INNER + 2 * SSD_GROUPS * SSD_DSTATE
CM_CH = 256
CM_KERNEL = 31
PEER_HEADS = 8
PEER_NKEYS = 128
PEER_EXPERTS = PEER_NKEYS * PEER_NKEYS
PEER_QDIM = 256
PEER_TOPK = 16
PEER_BLOCK = 128
IN_OFFSETS = (Q_LORA, Q_LORA + KV_LORA, Q_LORA + KV_LORA + QK_ROPE,
              Q_LORA + KV_LORA + QK_ROPE + SSD_INNER,
              Q_LORA + KV_LORA + QK_ROPE + SSD_INNER + SSD_CONV_DIM,
              Q_LORA + KV_LORA + QK_ROPE + SSD_INNER + SSD_CONV_DIM + 2 * SSD_HEADS)
IN_DIM = Q_LORA + KV_LORA + QK_ROPE + SSD_INNER + SSD_CONV_DIM + 2 * SSD_HEADS + 2 * CM_CH

kernel_name = 'hybrid_mla_ssd_conformer_peer_diffusion_step'

def rmsnorm(x, g):
    xf = x.astype(jnp.float32)
    y = xf * lax.rsqrt(jnp.mean(xf * xf, axis=-1, keepdims=True) + EPS)
    return (y * g.astype(jnp.float32)).astype(x.dtype)

def layernorm(x, g, b):
    xf = x.astype(jnp.float32)
    mu = jnp.mean(xf, axis=-1, keepdims=True)
    var = jnp.mean(jnp.square(xf - mu), axis=-1, keepdims=True)
    y = (xf - mu) * lax.rsqrt(var + EPS) * g.astype(jnp.float32) + b.astype(jnp.float32)
    return y.astype(x.dtype)

def axial_rope_tables(n_tokens):
    rows = n_tokens // GRID_W
    row = jnp.repeat(jnp.arange(rows, dtype=jnp.float32), GRID_W)
    col = jnp.tile(jnp.arange(GRID_W, dtype=jnp.float32), rows)
    inv = ROPE_THETA ** (-jnp.arange(ROPE_FREQS, dtype=jnp.float32) / ROPE_FREQS)
    ang = jnp.stack([row[:, None] * inv, col[:, None] * inv], axis=1)
    return jnp.cos(ang), jnp.sin(ang)

def apply_axial_rope(x, cos, sin):
    xs = x.reshape(x.shape[:-1] + (2, 2, ROPE_FREQS))
    x1, x2 = xs[..., 0, :], xs[..., 1, :]
    out = jnp.stack([x1 * cos - x2 * sin, x2 * cos + x1 * sin], axis=-2)
    return out.reshape(x.shape).astype(x.dtype)

def depthwise_conv(x, w, b):
    k, ch = w.shape
    y = lax.conv_general_dilated(x, w[:, None, :].astype(x.dtype), window_strides=(1,),
                                 padding=((k // 2, k // 2),), dimension_numbers=('NWC', 'WIO', 'NWC'),
                                 feature_group_count=ch)
    return y + b.astype(x.dtype)

def blocked_attention(q, k, v, scale):
    bsz, tq, nh, dq = q.shape
    nb = tq // ATTN_BLOCK
    qb = q.reshape(bsz, nb, ATTN_BLOCK, nh, dq).transpose(1, 0, 2, 3, 4)

    def one(qblk):
        s = jnp.einsum('bqhd,bkhd->bhqk', qblk, k).astype(jnp.float32) * scale
        p = jax.nn.softmax(s, axis=-1).astype(v.dtype)
        return jnp.einsum('bhqk,bkhd->bqhd', p, v)

    o = lax.map(one, qb)
    return o.transpose(1, 0, 2, 3, 4).reshape(bsz, tq, nh, v.shape[-1])

def mla_keys(ckv, kpe, w_ukv):
    bsz, t, _ = ckv.shape
    kv = jnp.einsum('btr,rf->btf', ckv, w_ukv).reshape(bsz, t, MLA_HEADS, QK_NOPE + V_HEAD)
    k_pe_h = jnp.broadcast_to(kpe[:, :, None, :], (bsz, t, MLA_HEADS, QK_ROPE)).astype(kv.dtype)
    return jnp.concatenate([kv[..., :QK_NOPE], k_pe_h], axis=-1), kv[..., QK_NOPE:]

def segsum(a):
    t = a.shape[-1]
    cs = jnp.cumsum(a, axis=-1)
    diff = cs[..., :, None] - cs[..., None, :]
    mask = jnp.tril(jnp.ones((t, t), dtype=bool))
    return jnp.where(mask, diff, -jnp.inf)

def ssd_scan(x, dt, a_neg, bm, cm, h0):
    b, l, h, p = x.shape
    g, n = bm.shape[-2:]
    nc, lc = l // SSD_CHUNK, SSD_CHUNK
    rep = h // g
    bh = jnp.repeat(bm.astype(jnp.float32), rep, axis=2).reshape(b, nc, lc, h, n)
    ch = jnp.repeat(cm.astype(jnp.float32), rep, axis=2).reshape(b, nc, lc, h, n)
    xdt = (x.astype(jnp.float32) * dt[..., None]).reshape(b, nc, lc, h, p)
    a = (dt * a_neg).reshape(b, nc, lc, h).transpose(0, 3, 1, 2)
    a_cum = jnp.cumsum(a, axis=-1)
    lmat = jnp.exp(segsum(a))
    scores = jnp.einsum('bclhn,bcshn->bhcls', ch, bh) * lmat
    y_diag = jnp.einsum('bhcls,bcshp->bclhp', scores, xdt)
    decay_states = jnp.exp(a_cum[..., -1:] - a_cum)
    states = jnp.einsum('bclhn,bhcl,bclhp->bchpn', bh, decay_states, xdt)
    states = jnp.concatenate([h0[:, None].astype(jnp.float32), states], axis=1)
    chunk_a = jnp.pad(a_cum[..., -1], ((0, 0), (0, 0), (1, 0)))
    decay_chunk = jnp.exp(segsum(chunk_a))
    new_states = jnp.einsum('bhzc,bchpn->bzhpn', decay_chunk, states)
    states, final = new_states[:, :-1], new_states[:, -1]
    y_off = jnp.einsum('bclhn,bchpn,bhcl->bclhp', ch, states, jnp.exp(a_cum))
    return (y_diag + y_off).reshape(b, l, h, p), final

def ssd_mixer(z, xbc, dt_raw, lp, h0):
    bsz, t, _ = z.shape
    xbc = jax.nn.silu(depthwise_conv(xbc, lp['ssd_conv_w'], lp['ssd_conv_b']))
    xs = xbc[..., :SSD_INNER].reshape(bsz, t, SSD_HEADS, SSD_HEADDIM)
    bm = xbc[..., SSD_INNER:SSD_INNER + SSD_GROUPS * SSD_DSTATE].reshape(bsz, t, SSD_GROUPS, SSD_DSTATE)
    cm = xbc[..., SSD_INNER + SSD_GROUPS * SSD_DSTATE:].reshape(bsz, t, SSD_GROUPS, SSD_DSTATE)
    dt = jax.nn.softplus(dt_raw.astype(jnp.float32) + lp['ssd_dt_bias'].astype(jnp.float32))
    a_neg = -jnp.exp(lp['ssd_a_log'].astype(jnp.float32))
    y_f, h_f = ssd_scan(xs, dt[:, :, 0], a_neg[0], bm, cm, h0[:, 0])
    y_b, h_b = ssd_scan(jnp.flip(xs, 1), jnp.flip(dt[:, :, 1], 1), a_neg[1], jnp.flip(bm, 1),
                        jnp.flip(cm, 1), h0[:, 1])
    y = y_f + jnp.flip(y_b, 1) + xs.astype(jnp.float32) * lp['ssd_d'].astype(jnp.float32)[:, None]
    y = y.reshape(bsz, t, SSD_INNER) * jax.nn.silu(z.astype(jnp.float32))
    y = rmsnorm(y, lp['ssd_norm_g'])
    return y.astype(z.dtype), jnp.stack([h_f, h_b], axis=1).astype(z.dtype)

def conv_module(u, lp):
    a, gt = jnp.split(u, 2, axis=-1)
    hcv = a * jax.nn.sigmoid(gt)
    hcv = depthwise_conv(hcv, lp['cm_dw_w'], lp['cm_dw_b'])
    hcv = layernorm(hcv, lp['cm_ln_g'], lp['cm_ln_b'])
    return jax.nn.silu(hcv)

def mixer(h, lp, rope, ctx):
    bsz, t, _ = h.shape
    proj = jnp.einsum('btd,df->btf', h, lp['w_in'])
    c_q, c_kv, k_pe, z, xbc, dt_raw, glu = jnp.split(proj, IN_OFFSETS, axis=-1)
    q = jnp.einsum('btr,rf->btf', rmsnorm(c_q, lp['q_norm_g']), lp['w_uq'])
    q = q.reshape(bsz, t, MLA_HEADS, QK_NOPE + QK_ROPE)
    q_nope, q_pe = q[..., :QK_NOPE], q[..., QK_NOPE:]
    c_kv = rmsnorm(c_kv, lp['kv_norm_g'])
    if rope is None:
        k_pe_used = k_pe
        h0 = jnp.zeros((bsz, 2, SSD_HEADS, SSD_HEADDIM, SSD_DSTATE), jnp.float32)
    else:
        cos, sin = rope
        q_pe = apply_axial_rope(q_pe, cos[:, None], sin[:, None])
        k_pe_used = apply_axial_rope(k_pe, cos, sin)
        h0 = ctx[2]
    k, v = mla_keys(c_kv, k_pe_used, lp['w_ukv'])
    if ctx is not None:
        k_c, v_c = mla_keys(ctx[0], ctx[1], lp['w_ukv'])
        k = jnp.concatenate([k_c.astype(k.dtype), k], axis=1)
        v = jnp.concatenate([v_c.astype(v.dtype), v], axis=1)
    attn = blocked_attention(jnp.concatenate([q_nope, q_pe], axis=-1), k, v, MLA_SCALE)
    attn = attn.reshape(bsz, t, MLA_OUT)
    y_ssd, h_fin = ssd_mixer(z, xbc, dt_raw.reshape(bsz, t, 2, SSD_HEADS), lp, h0)
    y_conv = conv_module(glu, lp)
    cat = jnp.concatenate([attn, y_ssd.astype(attn.dtype), y_conv.astype(attn.dtype)], axis=-1)
    out = jnp.einsum('btf,fd->btd', cat, lp['w_out'])
    ctx_out = (c_kv, k_pe, h_fin) if ctx is None else None
    return out, ctx_out

def peer_ffn(h, w_q, sub_keys, u_tab, v_tab):
    bsz, t, d = h.shape
    tok = h.reshape(-1, PEER_BLOCK, d)

    def one(hb):
        q = (hb @ w_q).reshape(PEER_BLOCK, PEER_HEADS, 2, PEER_QDIM // 2)
        s = jnp.einsum('thsk,snk->thsn', q, sub_keys).astype(jnp.float32)
        top_s, top_i = lax.top_k(s, PEER_TOPK)
        cand = top_s[..., 0, :, None] + top_s[..., 1, None, :]
        cand_idx = top_i[..., 0, :, None] * PEER_NKEYS + top_i[..., 1, None, :]
        best_s, best_j = lax.top_k(cand.reshape(PEER_BLOCK, PEER_HEADS, PEER_TOPK * PEER_TOPK), PEER_TOPK)
        idx = jnp.take_along_axis(cand_idx.reshape(PEER_BLOCK, PEER_HEADS, PEER_TOPK * PEER_TOPK), best_j, axis=-1)
        gate = jax.nn.softmax(best_s, axis=-1).astype(hb.dtype)
        act = jax.nn.gelu(jnp.einsum('thkd,td->thk', u_tab[idx], hb), approximate=False)
        return jnp.einsum('thk,thkd->td', gate * act, v_tab[idx])

    return lax.map(one, tok).reshape(bsz, t, d)

def trunk_layer(x, cond, lp, rope, ctx):
    m = jnp.einsum('bsd,df->bsf', jax.nn.silu(cond), lp['w_ada']) + lp['b_ada']
    sh1, sc1, g1, sh2, sc2, g2 = jnp.split(m, 6, axis=-1)
    hmix = rmsnorm(x, lp['norm1_g']) * (1 + sc1) + sh1
    mix, ctx_out = mixer(hmix, lp, rope, ctx)
    x = x + g1 * mix
    hff = rmsnorm(x, lp['norm2_g']) * (1 + sc2) + sh2
    x = x + g2 * peer_ffn(hff, lp['peer_wq'], lp['peer_keys'], lp['peer_u'], lp['peer_v'])
    return x, ctx_out

def setup_inputs(seed: int = 0) -> dict:
    key = jax.random.key(seed)
    ks = jax.random.split(key, 40)

    def nrm(i, shape, scale):
        return jax.random.normal(ks[i], shape, jnp.float32) * scale

    L, D = DEPTH, D_MODEL
    dt0 = jnp.exp(jax.random.uniform(ks[30], (L, 2, SSD_HEADS), jnp.float32, math.log(1e-3), math.log(1e-1)))
    return {
        'x_prompt': nrm(0, (BATCH, SEQ, D), 1.0),
        'x_sample': nrm(1, (DEC_BATCH, DEC_SEQ, D), 1.0),
        'cache_ckv': nrm(2, (DEC_BATCH, DEPTH, PAST_LEN, KV_LORA), 1.0),
        'cache_kpe': nrm(3, (DEC_BATCH, DEPTH, PAST_LEN, QK_ROPE), 1.0),
        'state_ssm': nrm(4, (DEC_BATCH, DEPTH, 2, SSD_HEADS, SSD_HEADDIM, SSD_DSTATE), 0.5),
        'c': nrm(5, (DEC_BATCH, D), 1.0),
        'c_ctx': nrm(6, (D,), 1.0),
        'norm1_g': 1.0 + nrm(7, (L, D), 0.02),
        'norm2_g': 1.0 + nrm(8, (L, D), 0.02),
        'w_ada': nrm(9, (L, D, 6 * D), 0.5 * D ** -0.5),
        'b_ada': nrm(10, (L, 6 * D), 0.02),
        'w_in': nrm(11, (L, D, IN_DIM), D ** -0.5),
        'q_norm_g': 1.0 + nrm(12, (L, Q_LORA), 0.02),
        'w_uq': nrm(13, (L, Q_LORA, MLA_HEADS * (QK_NOPE + QK_ROPE)), Q_LORA ** -0.5),
        'kv_norm_g': 1.0 + nrm(14, (L, KV_LORA), 0.02),
        'w_ukv': nrm(15, (L, KV_LORA, MLA_HEADS * (QK_NOPE + V_HEAD)), KV_LORA ** -0.5),
        'ssd_conv_w': nrm(16, (L, SSD_CONV, SSD_CONV_DIM), SSD_CONV ** -0.5),
        'ssd_conv_b': nrm(17, (L, SSD_CONV_DIM), 0.02),
        'ssd_dt_bias': dt0 + jnp.log(-jnp.expm1(-dt0)),
        'ssd_a_log': jnp.log(jax.random.uniform(ks[18], (L, 2, SSD_HEADS), jnp.float32, 1.0, 16.0)),
        'ssd_d': 1.0 + nrm(19, (L, SSD_HEADS), 0.1),
        'ssd_norm_g': 1.0 + nrm(20, (L, SSD_INNER), 0.02),
        'cm_dw_w': nrm(21, (L, CM_KERNEL, CM_CH), CM_KERNEL ** -0.5),
        'cm_dw_b': nrm(22, (L, CM_CH), 0.02),
        'cm_ln_g': 1.0 + nrm(23, (L, CM_CH), 0.02),
        'cm_ln_b': nrm(24, (L, CM_CH), 0.02),
        'w_out': nrm(25, (L, D_MIX, D), D_MIX ** -0.5),
        'peer_wq': nrm(26, (L, D, PEER_HEADS * PEER_QDIM), D ** -0.5),
        'peer_keys': nrm(27, (L, 2, PEER_NKEYS, PEER_QDIM // 2), (PEER_QDIM // 2) ** -0.5),
        'peer_u': nrm(28, (L, PEER_EXPERTS, D), D ** -0.5),
        'peer_v': nrm(29, (L, PEER_EXPERTS, D), PEER_HEADS ** -0.5),
        'final_g': 1.0 + nrm(31, (D,), 0.02),
    }

def reference(x_prompt, x_sample, cache_ckv, cache_kpe, state_ssm, c, c_ctx,
              norm1_g, norm2_g, w_ada, b_ada, w_in, q_norm_g, w_uq, kv_norm_g, w_ukv,
              ssd_conv_w, ssd_conv_b, ssd_dt_bias, ssd_a_log, ssd_d, ssd_norm_g,
              cm_dw_w, cm_dw_b, cm_ln_g, cm_ln_b, w_out,
              peer_wq, peer_keys, peer_u, peer_v, final_g):
    rope = axial_rope_tables(x_sample.shape[1])
    cond_ctx = c_ctx[None, None, :]
    cond_lat = c[:, None, :]
    yp, ys = x_prompt, x_sample
    ckv_list, kpe_list, ssm_list = [], [], []
    for l in range(DEPTH):
        lp = {
            'norm1_g': norm1_g[l], 'norm2_g': norm2_g[l], 'w_ada': w_ada[l], 'b_ada': b_ada[l],
            'w_in': w_in[l], 'q_norm_g': q_norm_g[l], 'w_uq': w_uq[l], 'kv_norm_g': kv_norm_g[l],
            'w_ukv': w_ukv[l], 'ssd_conv_w': ssd_conv_w[l], 'ssd_conv_b': ssd_conv_b[l],
            'ssd_dt_bias': ssd_dt_bias[l], 'ssd_a_log': ssd_a_log[l], 'ssd_d': ssd_d[l],
            'ssd_norm_g': ssd_norm_g[l], 'cm_dw_w': cm_dw_w[l], 'cm_dw_b': cm_dw_b[l],
            'cm_ln_g': cm_ln_g[l], 'cm_ln_b': cm_ln_b[l], 'w_out': w_out[l],
            'peer_wq': peer_wq[l], 'peer_keys': peer_keys[l], 'peer_u': peer_u[l], 'peer_v': peer_v[l],
        }
        yp, (ckv_l, kpe_l, ssm_l) = trunk_layer(yp, cond_ctx, lp, None, None)
        ckv_list.append(ckv_l)
        kpe_list.append(kpe_l)
        ssm_list.append(ssm_l)
        ys, _ = trunk_layer(ys, cond_lat, lp, rope, (cache_ckv[:, l], cache_kpe[:, l], state_ssm[:, l]))
    y_prompt = rmsnorm(yp, final_g)
    y_sample = rmsnorm(ys, final_g)
    new_ckv = jnp.stack(ckv_list, axis=1)
    new_kpe = jnp.stack(kpe_list, axis=1)
    new_ssm = jnp.stack(ssm_list, axis=1)
    return (y_prompt, y_sample, new_ckv, new_kpe, new_ssm)


_drawn_inputs = setup_inputs


def setup_inputs(seed=0):
    import zlib

    import numpy as np

    out = dict(_drawn_inputs(seed))
    spreads = {}
    factors = {'cache_ckv': 6.218,
     'cache_kpe': 8.0,
     'norm2_g': 4.472,
     'q_norm_g': 8.0,
     'kv_norm_g': 2.886,
     'ssd_norm_g': 5.11,
     'cm_dw_b': 4.955,
     'cm_ln_g': 5.549,
     'cm_ln_b': 8.0,
     'final_g': 2.894}
    for name, (base, spread) in spreads.items():
        noise = np.random.default_rng([zlib.crc32(name.encode()), seed]).standard_normal(out[name].shape)
        drawn = base * np.exp(spread * noise) if base else spread * noise
        out[name] = __import__('jax').numpy.asarray(drawn.astype(out[name].dtype))
    for name, factor in factors.items():
        out[name] = (out[name] * factor).astype(out[name].dtype)
    return out
```

```python
from contextlib import ExitStack

import numpy as np

import concourse.bass as bass
from concourse import mybir

ALU = mybir.AluOpType
ACT = mybir.ActivationFunctionType
AX = mybir.AxisListType
F32 = mybir.dt.float32
U32 = mybir.dt.uint32
I32 = mybir.dt.int32

P = 128
D = 1024
DC = D // P
L = 2
GROUP_BLOCKS = (1, 4)
FIRST_BLOCK = (0, 1)
NBLK = 5
KV_BLOCKS = (1, 5)
EPS = 1e-6
Q_LORA, KV_LORA, ROPE = 256, 128, 32
HEADS, NOPE, VH = 4, 64, 64
QK = NOPE + ROPE
MLA_SCALE = float(QK) ** -0.5
SH, SP_, SN, SG = 8, 64, 64, 2
INNER = SH * SP_
SCONV = 5
XBC = INNER + 2 * SG * SN
XCH = XBC // P
CM = 256
CMK = 31
IN_DIM = Q_LORA + KV_LORA + ROPE + INNER + XBC + 2 * SH + 2 * CM
OFF_Z = Q_LORA + KV_LORA + ROPE
OFF_X = OFF_Z + INNER
OFF_DT = OFF_X + XBC
OFF_G = OFF_DT + 2 * SH
TOK = OFF_Z + 2 * SH
PH, NK, TOPK = 8, 128, 16
NEXP = NK * NK
SLOTS = PH * TOPK
RING = 5
ROUNDS, TAIL = SLOTS // RING, SLOTS % RING
WU = 256
NW = 3
ADA_UNITS = 6 * D // WU
IN_UNITS, OUT_UNITS, PQ_UNITS = 9, D // WU, 2048 // WU
GROUP_UNITS = IN_UNITS + OUT_UNITS + PQ_UNITS
LAYER_UNITS = ADA_UNITS + 2 * GROUP_UNITS

PAR = {}
_at = 0
for _name, _n in (("n1", 8), ("n2", 8), ("qg", 2), ("cw", 30), ("cb", 6), ("sg", 4), ("dw", 62), ("db", 2),
                  ("lg", 2), ("lb", 2), ("kvg", 128), ("dtb", 16), ("alog", 16), ("sd", 8)):
    PAR[_name] = (_at, _at + _n)
    _at += _n
NPAR = _at
COLS = PAR["kvg"][0]
ROWS = NPAR - COLS
C_ID, C_UI, C_LI, C_LS, C_US, C_ONE, C_IOTA = range(7)


FULL_COUNTS = {
    "mod": (ADA_UNITS, 0), "modT": (16, 0),
    "n1": (2, 8), "pa": (2, 8), "pz": (2, 8), "px": (6, 6), "pg": (4, 4),
    "xt": (5, 5), "ct": (1, 4), "cT": (1, 4),
    "cs": (1, 4), "cb": (1, 4), "dd": (4, 16), "y": (2, 8), "yo": (2, 8), "st": (2, 8), "yT": (1, 4),
    "at": (1, 4), "kn": (4, 8), "v": (1, 5), "q": (1, 4), "qT": (1, 4),
    "sc": (4, 32), "pT": (4, 32), "o": (4, 16), "aT": (1, 4),
    "wo": (4, 16), "n2": (2, 8), "pq": (16, 16), "ps": (4, 16), "ht": (2, 8),
}


def ssd_steps(g):
    nb = GROUP_BLOCKS[g]
    return [(i % 2, i // 2 if i % 2 == 0 else nb - 1 - i // 2) for i in range(2 * nb)]


def attn_steps(g):
    return [(b, h) for b in range(GROUP_BLOCKS[g]) for h in range(HEADS)]


def key_segments(g):
    return [(0, P)] if g == 0 else [(0, P), (P, 512)]


def mod_steps():
    out, turned, waiting = [], 0, None
    for u in range(ADA_UNITS):
        out.append(("mod", u, u))
        if waiting is not None:
            out.append(("modT", turned, waiting))
            turned, waiting = turned + 1, None
        if (u // 4) not in (2, 5):
            waiting = u
    return out


BESIDE = {("n1", 7): 3, ("conv", 5): 2, ("cT", 3): 2, ("yT", 3): 2, ("v", 4): 2, ("n2", 7): 3}
for _stage, _of, _rows in (("pa", range(8), 1), ("pz", range(8), 1), ("px", range(6), 1), ("pg", range(4), 1),
                           ("taps", range(4, 30, 5), 1), ("st", range(8), 2), ("head", range(24), 1),
                           ("wo", range(16), 1), ("pq", range(16), 2)):
    BESIDE.update({(_stage, _i): _rows for _i in _of})


class Beside:
    LAST = SLOTS + 2

    def __init__(self, run):
        self.run, self.n, self.m = run, None, self.LAST + 1

    def start(self, n):
        self.n, self.m = n, 0

    def point(self, stage, i):
        for _ in range(BESIDE.get((stage, i), 0)):
            if self.m <= self.LAST:
                self.run(self.n, self.m)
                self.m += 1

    def rest(self):
        while self.m <= self.LAST:
            self.run(self.n, self.m)
            self.m += 1


def psum_order():
    out = []
    for l in range(L):
        out += [(s, l, 0, i) for s, i, _ in mod_steps()]
        for g in range(2):
            nb = GROUP_BLOCKS[g]
            seg = len(key_segments(g))
            for s in ("n1", "pa", "pz", "px", "pg", "xt"):
                out += [(s, l, g, i) for i in range(FULL_COUNTS[s][g])]
            for b in range(nb):
                out += [("cs", l, g, b), ("cb", l, g, b)]
            out += [("ct", l, g, b) for b in range(nb)]
            out += [("cT", l, g, b) for b in range(nb)]
            for i in range(2 * nb):
                out += [("dd", l, g, 2 * i), ("dd", l, g, 2 * i + 1), ("yo", l, g, i), ("y", l, g, i), ("st", l, g, i)]
            out += [("yT", l, g, b) for b in range(nb)]
            out += [("at", l, g, b) for b in range(nb)]
            out += [("kn", l, g, i) for i in range(HEADS * seg)]
            out += [("v", l, g, i) for i in range(KV_BLOCKS[g])]
            for b in range(nb):
                out += [("q", l, g, b), ("qT", l, g, b)]
                for h in range(HEADS + 2):
                    if h < HEADS:
                        out += [("sc", l, g, (b * HEADS + h) * seg + s) for s in range(seg)]
                    if 1 <= h <= HEADS:
                        out += [("pT", l, g, (b * HEADS + h - 1) * seg + s) for s in range(seg)]
                    if h >= 2:
                        out.append(("o", l, g, b * HEADS + h - 2))
                out.append(("aT", l, g, b))
            out += [("wo", l, g, i) for i in range(OUT_UNITS * nb)]
            out += [("n2", l, g, i) for i in range(2 * nb)]
            out += [("pq", l, g, i) for i in range(16)]
            for b in range(nb):
                out += [("ht", l, g, 2 * b), ("ht", l, g, 2 * b + 1)]
                out += [("ps", l, g, 4 * b + i) for i in range(4)]
    return out


def build(nc, x_in, ckvT_c, kpeT_c, h0, condT, w_ada, b_ada, w_in, w_uq, w_ukv, w_out, w_pq, keysT, uv, par, row, consts,
          rope, final_g, y_out, ckv_out, kpe_out, ssm_out):
    order = psum_order()
    place = {t: n for n, t in enumerate(order)}
    BANKS = 6
    with ExitStack() as ctx:
        def sb(name, shape, dt=F32):
            return ctx.enter_context(nc.sbuf_tensor(name, shape, dt))

        class Stage:
            def __init__(self, name, n=(1, 1), step=1):
                self.sem = ctx.enter_context(nc.semaphore(name))
                self.n, self.step = n, step

            def at(self, l, g=0, i=0):
                return self.sem, (l * sum(self.n) + (self.n[0] if g else 0) + i + 1) * self.step

        acc = ctx.enter_context(nc.psum_tensor("expert_acc", [P, 2, 512], F32))
        rot = ctx.enter_context(nc.psum_tensor("rotating", [P, BANKS, 512], F32))
        full = {s: Stage(f"{s}_full", n) for s, n in FULL_COUNTS.items()}
        free = {s: Stage(f"{s}_drained", n) for s, n in FULL_COUNTS.items()}

        def tile(s, l, g, i):
            return rot[:, place[(s, l, g, i)] % BANKS, :]

        X = sb("x", [P, NBLK, D])
        hT = sb("hT", [P, DC, 512])
        W = sb("w_ring", [P, NW, DC, WU])
        UV = sb("uv_ring", [P, RING, 2 * D])
        G = sb("gates", [P, 2, 2, D])
        C = sb("const_mats", [P, 7, P])
        rp = sb("rope_tables", [P, 4, 2, ROPE])
        pr = sb("params", [P, L, NPAR])
        wuq = sb("w_uq_s", [P, 2, HEADS * QK])
        wukv = sb("w_ukv_s", [P, HEADS * P])
        keys = sb("keys_s", [P, 2, NK])
        modc = sb("modc", [P, 4, DC, 2])
        sc_c = sb("silu_cond", [P, 2, DC, 2])
        st = sb("stats", [P, 64])
        nw = sb("newton", [P, 3, 8])
        dtt = sb("dt", [P, 3, 4, 16])
        ex = sb("decays", [P, 4, 48])
        aneg = sb("a_neg", [P, 16])
        idxs = sb("expert_index", [P, 2, SLOTS], U32)
        gat = sb("expert_gate", [P, 2, SLOTS])
        stage_ix = sb("index_stage", [P, RING], U32)
        dots = sb("u_dot", [P, RING])
        gel = sb("gelu", [P, RING])
        diag = sb("diag", [P, RING, P])
        bn = sb("conv_norm_stats", [P, 4, 8])
        htok_p = sb("prompt_rows", [P, D])
        arena = sb("arena", [P, 17100])

        used = [0]

        def at(off, *shape, dt=F32):
            n = int(np.prod(shape))
            used[0] = max(used[0], off + n)
            assert off + n <= 17100, off + n
            a = arena[:, off:off + n]
            if dt is not F32:
                a = a.bitcast(dt)
            if len(shape) > 1:
                names = " ".join(f"d{i}" for i in range(len(shape)))
                a = a.rearrange(f"p ({names}) -> p {names}", **{f"d{i}": s for i, s in enumerate(shape)})
            return a

        xn = [at(k * D, D) for k in range(2)]
        mrow = [at(2048 + k * WU, WU) for k in range(2)]
        brow = [at(2560 + k * WU, WU) for k in range(2)]
        junk = at(8384, D)
        tokA = at(0, 4, TOK)
        zs = at(1728, 4, INNER)
        xtok = at(3776, 4, 640)
        BC = at(6336, 2, 512)
        Cz = at(7360, 2, 512)
        yacc = at(8384, 4, INNER)
        xbcT = at(10432, XCH, 516)
        hcv = at(13528, 2, 542)
        cacc = at(14612, 2, 512)
        tz = [at(8384 + k * WU, WU) for k in range(2)]
        th = [at(8896 + k * 512, 512) for k in range(2)]
        ctok = [at(9920 + k * 256, 256) for k in range(2)]
        ctmp = [at(15636 + k * 512, 512) for k in range(2)]
        vtmp = [at(10432 + k * 256, 2, P) for k in range(2)]
        Em = [at(13504 + k * 1024, SH, P) for k in range(2)]
        xdt = at(12992, INNER)
        xdec = at(10432, INNER)
        gm = at(10944, 4, 2, 2, P)
        Sbd = at(15552, 2, INNER)
        ytmp = at(16576, INNER)
        KT = at(1728, HEADS, 640)
        V = at(4288, 5, HEADS * VH)
        QT = [at(5568 + k * 512, HEADS, P) for k in range(2)]
        ckvT = at(6592, 640)
        cqT = at(7232, 4, 2, P)
        kp96 = [at(8256 + k * QK, QK) for k in range(2)]
        qtok = [at(8448 + k * 384, HEADS * QK) for k in range(2)]
        Pm = [at(9216 + k * 640, 640) for k in range(2)]
        PT = [at(10496 + k * 640, 5, P) for k in range(2)]
        attn = [at(11776 + k * 256, 256) for k in range(2)]
        rtmp = at(12288, 2, HEADS, ROPE)
        otmp = [at(12800 + k * WU, WU) for k in range(2)]
        qT = at(0, 16, 512)
        scs = at(8192, 16, NK)
        cand = at(10240, PH, TOPK, TOPK)
        tv = at(12288, 16, TOPK)
        ti = at(12544, 16, TOPK, dt=U32)
        tif = at(12800, 16, TOPK)
        bv = at(13056, PH, TOPK)
        bj = at(13184, PH, TOPK, dt=U32)
        bi = at(13312, 2, PH, TOPK, dt=U32)
        bif = at(13568, 2, PH, TOPK)
        pick = at(13824, 2, PH, TOPK)
        gsum = at(14080, 2, PH)
        htok = [at(14336 + k * D, D) for k in range(2)]
        psum_out = at(16384, 512)

        w_loaded = [ctx.enter_context(nc.semaphore(f"w_loaded{k}")) for k in range(NW)]
        s_const = Stage("consts_loaded", step=16)
        s_x = Stage("x_loaded", step=16)
        s_lw = Stage("layer_weights_loaded", (1, 0), 16 * 3)
        s_brow = [Stage(f"b_ada_row_loaded{k}", (ADA_UNITS // 2, 0), 16) for k in range(2)]
        s_condt = Stage("cond_tanh", (1, 0))
        s_cond = Stage("cond_ready", (1, 0))
        s_modc = Stage("modulation_ready", (1, 0))
        s_cache = Stage("cache_loaded", (0, 1), 16 * 2)
        s_szero = Stage("state_cleared", (1, 1))
        s_state = Stage("state_loaded", (0, 1), 16 * 4)
        s_mout = Stage("mixer_outputs_stored", (1, 0), 16 * 6)
        s_out = Stage("outputs_stored", step=16)
        s_ss = {k: Stage(f"{k}_squares", (1, 1)) for k in ("n1", "n2", "aq", "ys", "nf")}
        s_rs = {k: Stage(f"{k}_rstd", (1, 1)) for k in ("n1", "n2", "nf")}
        s_xn = {k: Stage(f"{k}_scaled", (1, 4)) for k in ("n1", "n2", "ys")}
        s_ztanh = Stage("z_tanh", (2, 8))
        s_cconv = Stage("ssd_conv_done", (6, 6))
        s_ctanh = Stage("ssd_conv_tanh", (6, 6))
        s_silu = Stage("ssd_conv_silu", (6, 6))
        s_glu = Stage("conv_module_done")
        s_ctok = Stage("conv_norm_ready", (1, 4))
        s_carg = Stage("conv_silu_argument", (1, 4))
        s_cmt = Stage("conv_silu_tanh", (1, 4))
        s_dtv = Stage("dt_abs")
        s_dte = Stage("dt_log")
        s_a = Stage("a_ready")
        s_arow = Stage("decay_rows_ready", (2, 8))
        s_em = Stage("decay_mask_ready", (2, 8))
        s_xdt = Stage("xdt_ready", (2, 8))
        s_sup = Stage("state_updated", (2, 8))
        s_yg = Stage("y_gated", (1, 4))
        s_nrm = Stage("q_kv_normed", (1, 4))
        s_qr = Stage("q_roped", (0, 4))
        s_mx = Stage("score_max", (4, 16))
        s_attn = Stage("attn_rows_ready", (1, 4))
        s_bsub = Stage("gate_shifted", (1, 4))
        s_bexp = Stage("gate_exp", (1, 4))
        s_idx = Stage("experts_chosen", (1, 4))
        s_gate = Stage("gates_ready", (1, 4))
        s_pup = Stage("peer_added", (1, 4))
        s_fin = ctx.enter_context(nc.semaphore("final_rows_ready"))
        s_nfs = ctx.enter_context(nc.semaphore("final_scaled"))
        s_fg = Stage("final_g_loaded", step=16)
        s_gst = ctx.enter_context(nc.semaphore("indices_staged"))
        s_gat = [ctx.enter_context(nc.semaphore(f"rows_gathered{j}")) for j in range(RING)]
        s_issue = ctx.enter_context(nc.semaphore("gathers_issued"))
        s_dot = ctx.enter_context(nc.semaphore("u_dotted"))
        s_gel = ctx.enter_context(nc.semaphore("gelu_done"))
        s_dg = ctx.enter_context(nc.semaphore("diag_ready"))
        s_vs = ctx.enter_context(nc.semaphore("v_summed"))
        dve_chain = ctx.enter_context(nc.semaphore("dve_chain"))
        act_chain = ctx.enter_context(nc.semaphore("act_chain"))
        pool_chain = ctx.enter_context(nc.semaphore("pool_chain"))

        class Chain:
            def __init__(self, eng, sem):
                self.eng, self.sem, self.n = eng, sem, 0

            def __call__(self, ins):
                self.n += 1
                ins.then_inc(self.sem, 1)
                self.eng.wait_ge(self.sem, self.n)

        def blk(l, g, b):
            return l * NBLK + FIRST_BLOCK[g] + b

        def uses(j):
            return ROUNDS + (1 if j < TAIL else 0)

        def w_unit(l, g, kind, u):
            n = l * LAYER_UNITS
            if kind == "ada":
                return n + u
            return n + ADA_UNITS + g * GROUP_UNITS + {"in": 0, "out": IN_UNITS, "pq": IN_UNITS + OUT_UNITS}[kind] + u

        def unit_left(n):
            l, u = n // LAYER_UNITS, n % LAYER_UNITS
            if u < ADA_UNITS:
                return full["mod"].at(l, 0, u)
            g, u = (u - ADA_UNITS) // GROUP_UNITS, (u - ADA_UNITS) % GROUP_UNITS
            nb = GROUP_BLOCKS[g]
            if u < 2:
                return full["pa"].at(l, g, u * nb + nb - 1)
            if u < 4:
                return full["pz"].at(l, g, (u - 2) * nb + nb - 1)
            if u < 7:
                return full["px"].at(l, g, 2 * (u - 4) + 1)
            if u < IN_UNITS:
                return full["pg"].at(l, g, 2 * (u - 7) + 1)
            u -= IN_UNITS
            if u < OUT_UNITS:
                return full["wo"].at(l, g, u * nb + nb - 1)
            return full["pq"].at(l, g, 2 * (u - OUT_UNITS) + 1)

        block = ctx.enter_context(nc.Block())

        @block.sync
        def _(sp):
            sp.dma_start(C[:], consts.rearrange("c p m -> p c m")).then_inc(s_const.sem, 16)
            sp.dma_start(rp[:], rope.rearrange("b p c r -> p b c r")).then_inc(s_const.sem, 16)
            sp.dma_start(sc_c[:, 0], condT).then_inc(s_const.sem, 16)
            for l in range(L):
                sp.dma_start(pr[:, l, 0:COLS], par[l]).then_inc(s_const.sem, 16)
                sp.dma_start(pr[:, l, COLS:NPAR], row[l:l + 1, :].broadcast_to([P, ROWS])).then_inc(s_const.sem, 16)
            sp.dma_start(X[:], x_in.rearrange("(b p) d -> p b d", p=P)).then_inc(s_x.sem, 16)

            def load_w(n, src):
                if n >= NW:
                    sp.wait_ge(*unit_left(n - NW))
                for k in range(2):
                    sp.dma_start(W[:, n % NW, 4 * k:4 * k + 4, :],
                                 src[512 * k:512 * k + 512, :].rearrange("(c p) n -> p c n", p=P)).then_inc(w_loaded[n % NW], 16)

            for l in range(L):
                if l:
                    sp.wait_ge(*full["ps"].at(l - 1, 1, 15))
                    sp.wait_ge(*full["q"].at(l - 1, 1, 3))
                sp.dma_start(wuq[:], w_uq[l].rearrange("(c p) n -> p c n", p=P)).then_inc(s_lw.sem, 16)
                sp.dma_start(wukv[:], w_ukv[l]).then_inc(s_lw.sem, 16)
                sp.dma_start(keys[:], keysT[l].rearrange("k (s n) -> k s n", s=2)).then_inc(s_lw.sem, 16)
                if l:
                    sp.wait_ge(*s_pup.at(l - 1, 1, 3))
                for u in range(ADA_UNITS):
                    if u >= 2:
                        sp.wait_ge(*free["mod"].at(l, 0, u - 2))
                    sp.dma_start(brow[u % 2], b_ada[l:l + 1, u * WU:(u + 1) * WU].broadcast_to([P, WU])).then_inc(s_brow[u % 2].sem, 16)
                    load_w(w_unit(l, 0, "ada", u), w_ada[l, :, u * WU:(u + 1) * WU])
                for g in range(2):
                    for u in range(IN_UNITS):
                        n = w_unit(l, g, "in", u)
                        if u == 1:
                            sp.wait_ge(*unit_left(n - NW))
                            for lo, at_, width in ((256, 0, OFF_Z - 256), (OFF_DT, OFF_Z - 256, 2 * SH)):
                                sp.dma_start(W[:, n % NW, :, at_:at_ + width],
                                             w_in[l, :, lo:lo + width].rearrange("(c p) n -> p c n", p=P)).then_inc(w_loaded[n % NW], 16)
                            continue
                        lo = 0 if u == 0 else OFF_Z + (u - 2) * WU if u < 4 else OFF_X + (u - 4) * WU if u < 7 else OFF_G + (u - 7) * WU
                        load_w(n, w_in[l, :, lo:lo + WU])
                    if g == 1:
                        sp.wait_ge(*s_szero.at(l, 1))
                        for d in range(2):
                            for q in range(2):
                                sp.dma_start(Sbd[64 * q:64 * q + 64, d, 256 * q:256 * q + 256],
                                               h0[l, d, 64 * q:64 * q + 64, :]).then_inc(s_state.sem, 16)
                        sp.wait_ge(*full["yT"].at(l, 1, 3))
                        sp.wait_ge(*s_xn["ys"].at(l, 1, 3))
                        sp.dma_start(ckvT[:, 0:P], ckvT_c[l]).then_inc(s_cache.sem, 16)
                        sp.dma_start(KT[64:96, :, 0:P], kpeT_c[l].unsqueeze(1).broadcast_to([ROPE, HEADS, P])).then_inc(s_cache.sem, 16)
                    else:
                        for d in range(2):
                            sp.wait_ge(*s_sup.at(l, 0, d))
                            for q in range(2):
                                sp.dma_start(ssm_out[l, d, 64 * q:64 * q + 64, :],
                                               Sbd[64 * q:64 * q + 64, d, 256 * q:256 * q + 256]).then_inc(s_mout.sem, 16)
                        sp.wait_ge(*s_nrm.at(l, 0, 0))
                        sp.dma_start(ckv_out[l], tokA[:, 0, Q_LORA:Q_LORA + KV_LORA]).then_inc(s_mout.sem, 16)
                        sp.dma_start(kpe_out[l], tokA[:, 0, Q_LORA + KV_LORA:OFF_Z]).then_inc(s_mout.sem, 16)
                    for u in range(OUT_UNITS):
                        load_w(w_unit(l, g, "out", u), w_out[l, :, u * WU:(u + 1) * WU])
                    for u in range(PQ_UNITS):
                        load_w(w_unit(l, g, "pq", u), w_pq[l, :, u * WU:(u + 1) * WU])
            sp.wait_ge(*s_pup.at(L - 1, 1, 3))
            sp.dma_start(at(2 * D, D), final_g.rearrange("(a n) -> a n", a=1).broadcast_to([P, D])).then_inc(s_fg.sem, 16)
            for n in range(NBLK):
                sp.wait_ge(s_fin, n + 1)
                sp.dma_start(y_out[n * P:(n + 1) * P, :], X[:, n, :]).then_inc(s_out.sem, 16)
            sp.wait_ge(s_out.sem, NBLK * 16)
            sp.wait_ge(*s_mout.at(L - 1))

        @block.gpsimd
        def _(pool):
            for l in range(L):
                for g in range(2):
                    nb = GROUP_BLOCKS[g]
                    for b in range(nb):
                        n = blk(l, g, b)
                        base = n * SLOTS
                        pool.wait_ge(*s_idx.at(l, g, b))

                        def fetch(r, j):
                            first = isinstance(r, int) and r == 0
                            prev = base - SLOTS + (uses(j) - 1) * RING + j if first else base + r * RING + j - RING
                            if not first or n:
                                pool.wait_ge(s_vs, prev + 1)
                            pool.tensor_copy(stage_ix[:, j:j + 1], idxs[:, n % 2, bass.ds(r * RING + j, 1)]).then_inc(s_gst, 1)
                            pool.wait_ge(s_gst, base + r * RING + j + 1)
                            pool.sem_inc(s_issue, 1)
                            pool.indirect_dma_start(out=UV[:, j, :], out_offset=None, in_=uv,
                                                    in_offset=bass.IndirectOffsetOnAxis(ap=stage_ix[:, j:j + 1], axis=0)).then_inc(s_gat[j], 16)

                        for j in range(RING):
                            fetch(0, j)
                        with pool.Fori(1, ROUNDS) as r:
                            for j in range(RING):
                                fetch(r, j)
                        for j in range(TAIL):
                            fetch(ROUNDS, j)

        @block.tensor
        def _(pe):
            fills = iter(order)

            def fill(s, l, g, i):
                assert next(fills) == (s, l, g, i), (s, l, g, i)
                n = place[(s, l, g, i)]
                if n >= BANKS:
                    old = order[n - BANKS]
                    pe.wait_ge(*free[old[0]].at(*old[1:]))
                return rot[:, n % BANKS, :]

            def weights(l, g, kind, u):
                n = w_unit(l, g, kind, u)
                pe.wait_ge(w_loaded[n % NW], 32 * (n // NW + 1))
                return W[:, n % NW]

            def done(ins, s):
                ins.then_inc(full[s].sem, 1)

            def turn(out, src):
                return pe.transpose(out, src, C[:, C_ID, :])

            def norm_T(s, l, g):
                for b in range(GROUP_BLOCKS[g]):
                    pe.wait_ge(*s_xn[s].at(l, g, b))
                    for half in range(2):
                        t = fill(s, l, g, 2 * b + half)
                        for c in range(4):
                            k = 4 * half + c
                            ins = turn(t[:, c * P:(c + 1) * P], xn[b % 2][:, k * P:(k + 1) * P])
                        done(ins, s)

            def add_v(n, r, j, first=False, last=False):
                pe.wait_ge(s_dg, n * SLOTS + r * RING + j + 1)
                for k in range(2):
                    ins = pe.matmul(acc[:, k, :], diag[:, j, :], UV[:, j, D + 512 * k:D + 512 * k + 512],
                                    start=first, stop=last, skip_group_check=True)
                ins.then_inc(s_vs, 1)

            def add_round(n, r):
                if n and r == 0:
                    pe.wait_ge(s_pup.sem, n)
                for j in range(RING if r < ROUNDS else TAIL):
                    add_v(n, r, j, first=(r == 0 and j == 0), last=(r * RING + j == SLOTS - 1))

            def add_beside(n, m):
                if n and m == 2:
                    pe.wait_ge(s_pup.sem, n)
                if 2 <= m <= SLOTS + 1:
                    add_v(n, *divmod(m - 2, RING), first=(m == 2), last=(m == SLOTS + 1))

            beside = Beside(add_beside)

            pe.wait_ge(s_const.sem, 16 * 7)
            for l in range(L):
                pe.wait_ge(*s_cond.at(l))
                for s, i, u in mod_steps():
                    if s == "mod":
                        w = weights(l, 0, "ada", u)
                        t = fill("mod", l, 0, u)
                        for c in range(DC):
                            ins = pe.matmul(t[:, 0:WU], hT[:, c, 0:P], w[:, c, :], start=(c == 0), stop=(c == DC - 1))
                        done(ins, "mod")
                    else:
                        pe.wait_ge(*free["mod"].at(l, 0, u))
                        t = fill("modT", l, 0, i)
                        for c in range(2):
                            ins = turn(t[:, c * P:(c + 1) * P], mrow[i % 2][:, c * P:(c + 1) * P])
                        done(ins, "modT")

                for g in range(2):
                    nb = GROUP_BLOCKS[g]
                    T = nb * P
                    norm_T("n1", l, g)
                    beside.point("n1", 2 * nb - 1)
                    pe.wait_ge(*free["n1"].at(l, g, 2 * nb - 1))
                    for u in range(4):
                        w = weights(l, g, "in", u)
                        s = "pa" if u < 2 else "pz"
                        width = WU if u != 1 else TOK - 256
                        for b in range(nb):
                            t = fill(s, l, g, (u % 2) * nb + b)
                            for c in range(DC):
                                ins = pe.matmul(t[:, 0:width], hT[:, c, b * P:(b + 1) * P], w[:, c, 0:width],
                                                start=(c == 0), stop=(c == DC - 1))
                            done(ins, s)
                            beside.point(s, (u % 2) * nb + b)
                    for u in range(4, IN_UNITS):
                        w = weights(l, g, "in", u)
                        s, first = ("px", 4) if u < 7 else ("pg", 7)
                        for k in range(2):
                            t = fill(s, l, g, 2 * (u - first) + k)
                            for c in range(DC):
                                ins = pe.matmul(t[:, 0:T], w[:, c, k * P:(k + 1) * P], hT[:, c, 0:T],
                                                start=(c == 0), stop=(c == DC - 1))
                            done(ins, s)
                            beside.point(s, 2 * (u - first) + k)
                    for c in range(5):
                        pe.wait_ge(*s_silu.at(l, g, c))
                        t = fill("xt", l, g, c)
                        src = ctmp[c % 2] if c < 4 else BC[:, 0]
                        for b in range(nb):
                            ins = turn(t[:, b * P:(b + 1) * P], src[:, b * P:(b + 1) * P])
                        done(ins, "xt")
                    beside.point("conv", 5)
                    pe.wait_ge(*s_a.at(l, g))
                    pe.wait_ge(*s_silu.at(l, g, 5))
                    for b in range(nb):
                        t = fill("cs", l, g, b)
                        a = dtt[:, 1, b, :]
                        for m, lo, hi, src in ((C_UI, 0, 8, a[:, 0:8]), (C_LI, 8, 16, a[:, 8:16]), (C_LS, 16, 24, a[:, 0:8]),
                                               (C_US, 24, 32, a[:, 8:16]), (C_ONE, 32, 48, a)):
                            ins = pe.matmul(t[:, lo:hi], C[:, m, :], src, start=True, stop=True)
                        done(ins, "cs")
                        t = fill("cb", l, g, b)
                        done(pe.matmul(t[:, 0:2 * P], BC[:, 0, b * P:(b + 1) * P], Cz[:, :, b * P:(b + 1) * P],
                                       start=True, stop=True), "cb")
                    for k in range(CMK):
                        beside.point("taps", k)
                    pe.wait_ge(*s_glu.at(l, g))
                    for b in range(nb):
                        t = fill("ct", l, g, b)
                        for j in range(2):
                            ins = turn(t[:, j * P:(j + 1) * P], cacc[:, j, b * P:(b + 1) * P])
                        done(ins, "ct")
                    for b in range(nb):
                        pe.wait_ge(*s_ctok.at(l, g, b))
                        t = fill("cT", l, g, b)
                        for j in range(2):
                            ins = turn(t[:, j * P:(j + 1) * P], ctok[b % 2][:, j * P:(j + 1) * P])
                        done(ins, "cT")
                    beside.point("cT", nb - 1)
                    for i, (d, b) in enumerate(ssd_steps(g)):
                        pe.wait_ge(*s_arow.at(l, g, i))
                        for k in range(2):
                            t = fill("dd", l, g, 2 * i + k)
                            done(pe.matmul(t, C[:, C_US if d else C_LS, :], Em[i % 2][:, 4 * k:4 * k + 4, :],
                                           start=True, stop=True), "dd")
                        if i >= 2:
                            pe.wait_ge(*s_sup.at(l, g, i - 2))
                        else:
                            pe.wait_ge(*s_szero.at(l, g))
                            if g == 1:
                                pe.wait_ge(*s_state.at(l, 1))
                        t = fill("yo", l, g, i)
                        done(pe.matmul(t, BC[:, 1, b * P:(b + 1) * P], Sbd[:, d, :], start=True, stop=True), "yo")
                        pe.wait_ge(*s_xdt.at(l, g, i))
                        pe.wait_ge(*s_em.at(l, g, i))
                        t = fill("y", l, g, i)
                        for h in range(SH):
                            ins = pe.matmul(t[:, h * SP_:(h + 1) * SP_], Em[i % 2][:, h, :], xdt[:, h * SP_:(h + 1) * SP_],
                                            start=True, stop=True)
                        done(ins, "y")
                        t = fill("st", l, g, i)
                        done(pe.matmul(t, xtok[:, b, 512:640], xdec, start=True, stop=True), "st")
                        beside.point("st", i)
                    for b in range(nb):
                        pe.wait_ge(*s_xn["ys"].at(l, g, b))
                        t = fill("yT", l, g, b)
                        for j in range(4):
                            ins = turn(t[:, j * P:(j + 1) * P], yacc[:, b, j * P:(j + 1) * P])
                        done(ins, "yT")
                    beside.point("yT", nb - 1)
                    for b in range(nb):
                        pe.wait_ge(*s_nrm.at(l, g, b))
                        t = fill("at", l, g, b)
                        for j in range(3):
                            turn(t[:, j * P:(j + 1) * P], tokA[:, b, j * P:(j + 1) * P])
                        done(turn(t[0:QK, 3 * P:4 * P], kp96[b % 2]), "at")
                    pe.wait_ge(*s_lw.at(l))
                    if g == 1:
                        pe.wait_ge(*s_cache.at(l, 1))
                    pe.wait_ge(*free["at"].at(l, g, nb - 1))
                    segs = key_segments(g)
                    for h in range(HEADS):
                        for k, (lo, w_) in enumerate(segs):
                            t = fill("kn", l, g, h * len(segs) + k)
                            done(pe.matmul(t[0:NOPE, 0:w_], wukv[:, h * P:h * P + NOPE], ckvT[:, lo:lo + w_],
                                           start=True, stop=True), "kn")
                    for kb in range(KV_BLOCKS[g]):
                        t = fill("v", l, g, kb)
                        done(pe.matmul(t[:, 0:HEADS * VH], ckvT[:, kb * P:(kb + 1) * P],
                                       wukv[:].rearrange("p (h c) -> p h c", h=HEADS)[:, :, NOPE:], start=True, stop=True), "v")
                    beside.point("v", KV_BLOCKS[g] - 1)
                    for b in range(nb):
                        t = fill("q", l, g, b)
                        for j in range(2):
                            ins = pe.matmul(t[:, 0:HEADS * QK], cqT[:, b, j, :], wuq[:, j, :], start=(j == 0), stop=(j == 1))
                        done(ins, "q")
                        pe.wait_ge(*(s_qr if g else free["q"]).at(l, g, b))
                        t = fill("qT", l, g, b)
                        for h in range(HEADS):
                            ins = turn(t[0:QK, h * P:(h + 1) * P], qtok[b % 2][:, h * QK:(h + 1) * QK])
                        done(ins, "qT")
                        pe.wait_ge(*free["qT"].at(l, g, b))
                        if b == 0:
                            pe.wait_ge(*free["kn"].at(l, g, HEADS * len(segs) - 1))
                            pe.wait_ge(*free["v"].at(l, g, KV_BLOCKS[g] - 1))
                        for h in range(HEADS + 2):
                            n = b * HEADS + h
                            if h < HEADS:
                                for k, (lo, w_) in enumerate(segs):
                                    t = fill("sc", l, g, n * len(segs) + k)
                                    done(pe.matmul(t[:, 0:w_], QT[b % 2][0:QK, h, :], KT[0:QK, h, lo:lo + w_],
                                                   start=True, stop=True), "sc")
                            if 1 <= h <= HEADS:
                                for k, (lo, w_) in enumerate(segs):
                                    pe.wait_ge(*free["sc"].at(l, g, (n - 1) * len(segs) + k))
                                    t = fill("pT", l, g, (n - 1) * len(segs) + k)
                                    for c in range(w_ // P):
                                        ins = turn(t[:, c * P:(c + 1) * P], Pm[(n - 1) % 2][:, lo + c * P:lo + (c + 1) * P])
                                    done(ins, "pT")
                            if h >= 2:
                                m = n - 2
                                pe.wait_ge(*free["pT"].at(l, g, m * len(segs) + len(segs) - 1))
                                t = fill("o", l, g, m)
                                for c in range(KV_BLOCKS[g]):
                                    ins = pe.matmul(t[:, 0:VH], PT[m % 2][:, c, :], V[:, c, (h - 2) * VH:(h - 1) * VH],
                                                    start=(c == 0), stop=(c == KV_BLOCKS[g] - 1))
                                done(ins, "o")
                            beside.point("head", b * (HEADS + 2) + h)
                        pe.wait_ge(*s_attn.at(l, g, b))
                        t = fill("aT", l, g, b)
                        for j in range(2):
                            ins = turn(t[:, j * P:(j + 1) * P], attn[b % 2][:, j * P:(j + 1) * P])
                        done(ins, "aT")
                    for s in ("aT", "yT", "cT"):
                        pe.wait_ge(*free[s].at(l, g, nb - 1))
                    for u in range(OUT_UNITS):
                        w = weights(l, g, "out", u)
                        for b in range(nb):
                            t = fill("wo", l, g, u * nb + b)
                            for c in range(DC):
                                ins = pe.matmul(t[:, 0:WU], hT[:, c, b * P:(b + 1) * P], w[:, c, :],
                                                start=(c == 0), stop=(c == DC - 1))
                            done(ins, "wo")
                            beside.point("wo", u * nb + b)
                    norm_T("n2", l, g)
                    beside.point("n2", 2 * nb - 1)
                    pe.wait_ge(*free["n2"].at(l, g, 2 * nb - 1))
                    for u in range(PQ_UNITS):
                        w = weights(l, g, "pq", u)
                        for k in range(2):
                            t = fill("pq", l, g, 2 * u + k)
                            for c in range(DC):
                                ins = pe.matmul(t[:, 0:T], w[:, c, k * P:(k + 1) * P], hT[:, c, 0:T],
                                                start=(c == 0), stop=(c == DC - 1))
                            done(ins, "pq")
                            beside.point("pq", 2 * u + k)
                    pe.wait_ge(*free["pq"].at(l, g, 15))

                    def score_block(b):
                        for half in range(2):
                            t = fill("ht", l, g, 2 * b + half)
                            for c in range(4):
                                ins = turn(t[:, c * P:(c + 1) * P], hT[:, 4 * half + c, b * P:(b + 1) * P])
                            done(ins, "ht")
                        for k in range(4):
                            t = fill("ps", l, g, 4 * b + k)
                            for m in range(4):
                                ins = pe.matmul(t[:, m * P:(m + 1) * P], qT[:, 4 * k + m, b * P:(b + 1) * P],
                                                keys[:, m % 2, :], start=True, stop=True)
                            done(ins, "ps")

                    score_block(0)
                    if g == 0:
                        beside.start(blk(l, 0, 0))
                        continue
                    beside.rest()
                    for b in range(nb):
                        if b + 1 < nb:
                            score_block(b + 1)
                        n = blk(l, g, b)
                        add_round(n, 0)
                        with pe.Fori(1, ROUNDS) as r:
                            for j in range(RING):
                                add_v(n, r, j)
                        if TAIL:
                            add_round(n, ROUNDS)

        @block.scalar
        def _(act):
            chain = Chain(act, act_chain)

            def tile_of(s, l, g, i):
                act.wait_ge(*full[s].at(l, g, i))
                return tile(s, l, g, i)

            def norm_rows(s, l, g, rows):
                nb = GROUP_BLOCKS[g]
                for b in range(nb):
                    ins = nc.scalar.activation(junk, rows(b), ACT.Square, accum_out=st[:, b:b + 1])
                    if b == nb - 1:
                        ins.then_inc(s_ss[s].sem, 1)
                    else:
                        chain(ins)
                act.wait_ge(*s_rs[s].at(l, g))
                for b in range(nb):
                    if b >= 2:
                        act.wait_ge(*full[s].at(l, g, 2 * (b - 2) + 1))
                    nc.scalar.activation(xn[b % 2], rows(b), ACT.Copy, scale=st[:, 24 + b:25 + b]).then_inc(s_xn[s].sem, 1)

            def gelu(n, r, j):
                act.wait_ge(s_dot, n * SLOTS + r * RING + j + 1)
                nc.scalar.activation(gel[:, j:j + 1], dots[:, j:j + 1], ACT.Gelu).then_inc(s_gel, 1)

            def gelu_round(n, r):
                for j in range(RING if r < ROUNDS else TAIL):
                    gelu(n, r, j)

            def gelu_beside(n, m):
                if m < SLOTS:
                    gelu(n, *divmod(m, RING))

            beside = Beside(gelu_beside)

            act.wait_ge(s_const.sem, 16 * 7)
            act.wait_ge(s_x.sem, 16)
            for l in range(L):
                nc.scalar.activation(sc_c[:, 1], sc_c[:, 0], ACT.Tanh, scale=0.5).then_inc(s_condt.sem, 1)
                chain(nc.scalar.activation(aneg[:], pr[:, l, slice(*PAR["alog"])], ACT.Exp))
                for g in range(2):
                    nb = GROUP_BLOCKS[g]
                    T = nb * P
                    seg = len(key_segments(g))
                    if g:
                        act.wait_ge(*s_gate.at(l, 0, 0))
                    elif l:
                        act.wait_ge(*s_pup.at(l - 1, 1, 3))
                    norm_rows("n1", l, g, lambda b: X[:, FIRST_BLOCK[g] + b, :])
                    beside.point("n1", 2 * nb - 1)
                    for i in range(2 * nb):
                        t = tile_of("pa", l, g, i)
                        u, b = i // nb, i % nb
                        w_ = WU if u == 0 else TOK - 256
                        nc.scalar.activation(tokA[:, b, u * WU:u * WU + w_], t[:, 0:w_], ACT.Copy).then_inc(free["pa"].sem, 1)
                        beside.point("pa", i)
                    for i in range(2 * nb):
                        t = tile_of("pz", l, g, i)
                        if i >= 2:
                            act.wait_ge(*free["pz"].at(l, g, i - 2))
                        nc.scalar.activation(tz[i % 2], t[:, 0:WU], ACT.Tanh, scale=0.5).then_inc(s_ztanh.sem, 1)
                        beside.point("pz", i)
                    for i in range(6):
                        t = tile_of("px", l, g, i)
                        nc.scalar.activation(xbcT[:, i, 2:2 + T], t[:, 0:T], ACT.Copy).then_inc(free["px"].sem, 1)
                        beside.point("px", i)
                    for i in range(4):
                        t = tile_of("pg", l, g, i)
                        if i < 2:
                            nc.scalar.activation(hcv[:, i, 15:15 + T], t[:, 0:T], ACT.Copy).then_inc(free["pg"].sem, 1)
                        else:
                            nc.scalar.activation(cacc[:, i - 2, 0:T], t[:, 0:T], ACT.Tanh, scale=0.5).then_inc(free["pg"].sem, 1)
                        beside.point("pg", i)
                    for c in range(7):
                        if c < 6:
                            act.wait_ge(*s_cconv.at(l, g, c))
                            if c >= 2:
                                act.wait_ge(*s_silu.at(l, g, c - 2))
                            nc.scalar.activation(th[c % 2][:, 0:T], ctmp[c % 2][:, 0:T] if c < 4 else BC[:, c - 4, 0:T],
                                                 ACT.Tanh).then_inc(s_ctanh.sem, 1)
                        if 1 <= c <= 5:
                            t = tile_of("xt", l, g, c - 1)
                            nc.scalar.activation(xtok[:, 0:nb, (c - 1) * P:c * P], t[:, 0:T].rearrange("p (b m) -> p b m", b=nb),
                                                 ACT.Copy).then_inc(free["xt"].sem, 1)
                    beside.point("conv", 5)
                    act.wait_ge(*s_dtv.at(l, g))
                    chain(nc.scalar.activation(dtt[:, 2, 0:nb, :], dtt[:, 2, 0:nb, :], ACT.Exp, scale=-1.0))
                    nc.scalar.activation(dtt[:, 2, 0:nb, :], dtt[:, 2, 0:nb, :], ACT.Ln, bias=1.0).then_inc(s_dte.sem, 1)
                    for b in range(nb):
                        t = tile_of("cs", l, g, b)
                        nc.scalar.activation(ex[:, b, :], t[:, 0:48], ACT.Exp).then_inc(free["cs"].sem, 1)
                    for k in range(CMK):
                        beside.point("taps", k)
                    for b in range(nb):
                        act.wait_ge(*s_carg.at(l, g, b))
                        if b >= 2:
                            act.wait_ge(*free["cT"].at(l, g, b - 2))
                        nc.scalar.activation(th[b % 2][:, 0:256], vtmp[b % 2].rearrange("p j m -> p (j m)"), ACT.Tanh).then_inc(s_cmt.sem, 1)
                    beside.point("cT", nb - 1)
                    for i in range(2 * nb):
                        for k in range(2):
                            t = tile_of("dd", l, g, 2 * i + k)
                            if k == 0:
                                act.wait_ge(*full["dd"].at(l, g, 2 * i + 1))
                            nc.scalar.activation(Em[i % 2][:, 4 * k:4 * k + 4, :].rearrange("p h m -> p (h m)"), t,
                                                 ACT.Exp).then_inc(free["dd"].sem, 1)
                        beside.point("st", i)
                    for b in range(nb):
                        act.wait_ge(*s_yg.at(l, g, b))
                        ins = nc.scalar.activation(xdt, yacc[:, b, :], ACT.Square, accum_out=st[:, 16 + b:17 + b])
                        if b == nb - 1:
                            ins.then_inc(s_ss["ys"].sem, 1)
                        else:
                            chain(ins)
                    for b in range(nb):
                        t = tile_of("yT", l, g, b)
                        for j in range(4):
                            k = PAR["sg"][0] + j
                            ins = nc.scalar.activation(hT[:, 2 + j, b * P:(b + 1) * P], t[:, j * P:(j + 1) * P], ACT.Copy,
                                                       scale=pr[:, l, k:k + 1])
                        ins.then_inc(free["yT"].sem, 1)
                    beside.point("yT", nb - 1)
                    for b in range(nb):
                        chain(nc.scalar.activation(xdt[:, 0:256], tokA[:, b, 0:256], ACT.Square, accum_out=st[:, 8 + 2 * b:9 + 2 * b]))
                        ins = nc.scalar.activation(xdt[:, 0:128], tokA[:, b, 256:384], ACT.Square, accum_out=st[:, 9 + 2 * b:10 + 2 * b])
                        if b == nb - 1:
                            ins.then_inc(s_ss["aq"].sem, 1)
                        else:
                            chain(ins)
                    KO = P if g else 0
                    for b in range(nb):
                        t = tile_of("at", l, g, b)
                        for j in range(2):
                            k = PAR["qg"][0] + j
                            nc.scalar.activation(cqT[:, b, j, :], t[:, j * P:(j + 1) * P], ACT.Copy, scale=pr[:, l, k:k + 1])
                        nc.scalar.activation(ckvT[:, KO + b * P:KO + (b + 1) * P], t[:, 2 * P:3 * P], ACT.Copy)
                        for h in range(HEADS):
                            ins = nc.scalar.activation(KT[64:96, h, KO + b * P:KO + (b + 1) * P], t[64:96, 3 * P:4 * P], ACT.Copy)
                        ins.then_inc(free["at"].sem, 1)
                    segs = key_segments(g)
                    for h in range(HEADS):
                        for k, (lo, w_) in enumerate(segs):
                            t = tile_of("kn", l, g, h * seg + k)
                            nc.scalar.activation(KT[0:64, h, lo:lo + w_], t[0:64, 0:w_], ACT.Copy).then_inc(free["kn"].sem, 1)
                    beside.point("v", KV_BLOCKS[g] - 1)
                    for b in range(nb):
                        t = tile_of("q", l, g, b)
                        if b >= 2:
                            act.wait_ge(*full["qT"].at(l, g, b - 2))
                        nc.scalar.activation(qtok[b % 2], t[:, 0:HEADS * QK], ACT.Copy).then_inc(free["q"].sem, 1)
                        t = tile_of("qT", l, g, b)
                        if b >= 2:
                            act.wait_ge(*full["sc"].at(l, g, (b - 1) * HEADS * seg - 1))
                        nc.scalar.activation(QT[b % 2][0:QK].rearrange("p h m -> p (h m)"), t[0:QK, :], ACT.Copy).then_inc(free["qT"].sem, 1)
                        for h in range(HEADS + 2):
                            if h >= HEADS:
                                beside.point("head", b * (HEADS + 2) + h)
                                continue
                            n = b * HEADS + h
                            act.wait_ge(*s_mx.at(l, g, n))
                            if n >= 2:
                                act.wait_ge(*full["pT"].at(l, g, (n - 1) * seg - 1))
                                act.wait_ge(*free["o"].at(l, g, n - 2))
                            for k, (lo, w_) in enumerate(segs):
                                t = tile_of("sc", l, g, n * seg + k)
                                c = 48 + (n % 2) * 2 + k
                                nc.scalar.activation(Pm[n % 2][:, lo:lo + w_], t[:, 0:w_], ACT.Exp, scale=MLA_SCALE,
                                                     bias=st[:, 56 + n % 2:57 + n % 2],
                                                     accum_out=st[:, c:c + 1]).then_inc(free["sc"].sem, 1)
                            beside.point("head", b * (HEADS + 2) + h)
                        t = tile_of("aT", l, g, b)
                        nc.scalar.activation(hT[:, 0:2, b * P:(b + 1) * P], t[:, 0:256].rearrange("p (j m) -> p j m", j=2),
                                             ACT.Copy).then_inc(free["aT"].sem, 1)
                    for i in range(OUT_UNITS * nb):
                        beside.point("wo", i)
                    act.wait_ge(*free["wo"].at(l, g, OUT_UNITS * nb - 1))
                    act.wait_ge(*s_mout.at(l))
                    norm_rows("n2", l, g, lambda b: X[:, FIRST_BLOCK[g] + b, :])
                    beside.point("n2", 2 * nb - 1)
                    act.wait_ge(*free["n2"].at(l, g, 2 * nb - 1))
                    for i in range(16):
                        t = tile_of("pq", l, g, i)
                        nc.scalar.activation(qT[:, i, 0:T], t[:, 0:T], ACT.Copy).then_inc(free["pq"].sem, 1)
                        beside.point("pq", i)

                    def drain_scores(b):
                        for half in range(2):
                            t = tile_of("ht", l, g, 2 * b + half)
                            if b >= 2 and half == 0:
                                act.wait_ge(s_dot, (blk(l, g, b) - 1) * SLOTS)
                            nc.scalar.activation((htok[b % 2] if g else htok_p[:])[:, 512 * half:512 * half + 512], t, ACT.Copy).then_inc(free["ht"].sem, 1)
                        for k in range(4):
                            t = tile_of("ps", l, g, 4 * b + k)
                            if b and k == 0:
                                act.wait_ge(*s_idx.at(l, g, b - 1))
                            nc.scalar.activation(scs[:, 4 * k:4 * k + 4, :].rearrange("p s n -> p (s n)"), t, ACT.Copy).then_inc(free["ps"].sem, 1)

                    def gate_exp(b):
                        act.wait_ge(*s_bsub.at(l, g, b))
                        nc.scalar.activation(bv, bv, ACT.Exp).then_inc(s_bexp.sem, 1)

                    drain_scores(0)
                    gate_exp(0)
                    if g == 0:
                        beside.start(blk(l, 0, 0))
                        continue
                    beside.rest()
                    for b in range(nb):
                        if b + 1 < nb:
                            drain_scores(b + 1)
                        n = blk(l, g, b)
                        with act.Fori(0, ROUNDS) as r:
                            for j in range(RING):
                                gelu(n, r, j)
                        gelu_round(n, ROUNDS)
                        if b + 1 < nb:
                            gate_exp(b + 1)
            act.wait_ge(s_pup.sem, L * NBLK)
            for n in range(NBLK):
                chain(nc.scalar.activation(at(3 * D, D), X[:, n, :], ACT.Square, accum_out=st[:, n:n + 1]))
            act.wait_ge(s_fg.sem, 16)
            nc.scalar.activation(at(3 * D, 1), st[:, 0:1], ACT.Copy).then_inc(s_nfs, 1)

        @block.vector
        def _(dve):
            chain = Chain(dve, dve_chain)
            V_ = nc.vector

            def tile_of(s, l, g, i):
                dve.wait_ge(*full[s].at(l, g, i))
                return tile(s, l, g, i)

            def par_(l, name, i=0, n=1):
                a = PAR[name][0] + i
                return pr[:, l, a:a + n]

            def rsqrt(out, src, scale):
                k = src.shape[1]
                v, t = nw[:, 0, 0:k], nw[:, 1, 0:k]
                chain(V_.tensor_scalar(v, src, scale, EPS, ALU.mult, ALU.add))
                chain(V_.tensor_scalar(out.bitcast(I32), v.bitcast(I32), -0.5, 1597463007.0, ALU.mult, ALU.add))
                for _ in range(3):
                    chain(V_.tensor_tensor(t, out, out, ALU.mult))
                    chain(V_.tensor_tensor(t, t, v, ALU.mult))
                    chain(V_.tensor_scalar(t, t, -0.5, 1.5, ALU.mult, ALU.add))
                    chain(V_.tensor_tensor(out, out, t, ALU.mult))

            def norm_cols(s, l, g, shift, scale):
                nb = GROUP_BLOCKS[g]
                dve.wait_ge(*s_ss[s].at(l, g))
                rsqrt(st[:, 24:24 + nb], st[:, 0:nb], 1.0 / D)
                V_.tensor_copy(nw[:, 2, 0:1], nw[:, 0, 0:1]).then_inc(s_rs[s].sem, 1)
                for b in range(nb):
                    for half in range(2):
                        t = tile_of(s, l, g, 2 * b + half)
                        for c in range(4):
                            k = 4 * half + c
                            ins = V_.tensor_scalar(hT[:, k, b * P:(b + 1) * P], t[:, c * P:(c + 1) * P],
                                                   modc[:, scale, k, g:g + 1], modc[:, shift, k, g:g + 1], ALU.mult, ALU.add)
                        ins.then_inc(free[s].sem, 1)

            def rows_of(n):
                return htok[(n % NBLK - 1) % 2] if n % NBLK else htok_p[:]

            def dot(n, r, j):
                dve.wait_ge(s_gat[j], (n * uses(j) + r + 1) * 16)
                V_.tensor_tensor_reduce(UV[:, j, 0:D], UV[:, j, 0:D], rows_of(n), 1.0, 0.0, ALU.mult, ALU.add,
                                        dots[:, j:j + 1]).then_inc(s_dot, 1)

            def weigh(n, r, j):
                dve.wait_ge(s_gel, n * SLOTS + r * RING + j + 1)
                V_.tensor_scalar(diag[:, j, :], C[:, C_ID, :], gat[:, n % 2, bass.ds(r * RING + j, 1)], gel[:, j:j + 1],
                                 ALU.mult, ALU.mult).then_inc(s_dg, 1)

            def add_peer(n):
                g = 1 if n % NBLK else 0
                tmp = psum_out if g else htok_p[:, 0:512]
                dve.wait_ge(s_vs, (n + 1) * SLOTS)
                for k in range(2):
                    x = X[:, n % NBLK, 512 * k:512 * k + 512]
                    chain(V_.tensor_tensor(tmp, acc[:, k, :], G[:, 1, g, 512 * k:512 * k + 512], ALU.mult))
                    ins = V_.tensor_tensor(x, x, tmp, ALU.add)
                    if k == 0:
                        chain(ins)
                ins.then_inc(s_pup.sem, 1)

            def dot_beside(n, m):
                if m < SLOTS:
                    dot(n, *divmod(m, RING))
                if 1 <= m <= SLOTS:
                    weigh(n, *divmod(m - 1, RING))
                if m == SLOTS + 2:
                    add_peer(n)

            beside = Beside(dot_beside)

            dve.wait_ge(s_const.sem, 16 * 7)
            dve.wait_ge(s_x.sem, 16)
            for l in range(L):
                for name in ("cw", "cb", "dw", "lg", "lb"):
                    lo, hi = PAR[name]
                    chain(V_.tensor_scalar(pr[:, l, lo:hi], pr[:, l, lo:hi], 0.5, None, ALU.mult))
            for l in range(L):
                dve.wait_ge(*s_condt.at(l))
                chain(V_.scalar_tensor_tensor(sc_c[:, 1], sc_c[:, 1], 1.0, sc_c[:, 0], ALU.add, ALU.mult))
                chain(V_.tensor_scalar(sc_c[:, 1], sc_c[:, 1], 0.5, None, ALU.mult))
                for k in range(2):
                    ins = V_.tensor_copy(hT[:, :, 64 * k:64 * k + 64], sc_c[:, 1, :, k:k + 1].broadcast_to([P, DC, 64]))
                ins.then_inc(s_cond.sem, 1)
                which = {0: 0, 1: 1, 3: 2, 4: 3}
                turned = 0
                for s, i, u in mod_steps():
                    if s == "mod":
                        t = tile_of("mod", l, 0, u)
                        dve.wait_ge(*s_brow[u % 2].at(l, 0, u // 2))
                        part, col = u // 4, (u % 4) * WU
                        if part in (2, 5):
                            for k in range(2):
                                for q in range(2):
                                    ins = V_.tensor_tensor(G[64 * q:64 * q + 64, part // 3, k, col:col + WU],
                                                           t[64 * k:64 * k + 64, 0:WU], brow[u % 2][64 * k:64 * k + 64, :], ALU.add)
                        else:
                            if turned >= 2:
                                dve.wait_ge(*full["modT"].at(l, 0, turned - 2))
                            ins = V_.tensor_tensor(mrow[turned % 2], t[:, 0:WU], brow[u % 2], ALU.add)
                            turned += 1
                        ins.then_inc(free["mod"].sem, 1)
                    else:
                        t = tile_of("modT", l, 0, i)
                        k = 2 * (u % 4)
                        V_.tensor_copy(modc[:, which[u // 4], k:k + 2, :],
                                       t[:, 0:2 * P].rearrange("p (k m) -> p k m", k=2)[:, :, 0:P:64]).then_inc(free["modT"].sem, 1)
                dve.wait_ge(*free["modT"].at(l, 0, 15))
                for m, name in ((1, "n1"), (3, "n2")):
                    chain(V_.scalar_tensor_tensor(modc[:, m], modc[:, m], 1.0,
                                                  par_(l, name, 0, 8).unsqueeze(2).broadcast_to([P, DC, 2]), ALU.add, ALU.mult))

                for g in range(2):
                    nb = GROUP_BLOCKS[g]
                    T = nb * P
                    seg = len(key_segments(g))
                    norm_cols("n1", l, g, 0, 1)
                    beside.point("n1", 2 * nb - 1)
                    for i in range(2 * nb):
                        beside.point("pa", i)
                    for i in range(2 * nb):
                        u, b = i // nb, i % nb
                        dve.wait_ge(*s_ztanh.at(l, g, i))
                        V_.scalar_tensor_tensor(zs[:, b, u * WU:(u + 1) * WU], tz[i % 2], 1.0, tile("pz", l, g, i)[:, 0:WU],
                                                ALU.add, ALU.mult).then_inc(free["pz"].sem, 1)
                        beside.point("pz", i)
                    V_.memset(xbcT[:, :, 0:2], 0.0)
                    V_.memset(xbcT[:, :, 2 + T:4 + T], 0.0)
                    V_.memset(hcv[:, :, 0:15], 0.0)
                    V_.memset(hcv[:, :, 15 + T:30 + T], 0.0)
                    chain(V_.memset(Cz[:], 0.0))
                    for c in range(7):
                        if c < 6:
                            dve.wait_ge(*free["px"].at(l, g, c))
                            if 2 <= c < 4:
                                dve.wait_ge(*full["xt"].at(l, g, c - 2))
                            o = ctmp[c % 2][:, 0:T] if c < 4 else BC[:, c - 4, 0:T]
                            chain(V_.tensor_scalar(o, xbcT[:, c, 0:T], par_(l, "cw", c * SCONV), par_(l, "cb", c), ALU.mult, ALU.add))
                            for k in range(1, SCONV):
                                ins = V_.scalar_tensor_tensor(o, xbcT[:, c, k:k + T], par_(l, "cw", c * SCONV + k), o, ALU.mult, ALU.add)
                                if k < SCONV - 1:
                                    chain(ins)
                            ins.then_inc(s_cconv.sem, 1)
                        for s, i in {0: [("px", i) for i in range(3)], 1: [("px", i) for i in range(3, 6)] + [("pg", i) for i in range(4)]}.get(c, []):
                            beside.point(s, i)
                        if c >= 1:
                            m = c - 1
                            o = ctmp[m % 2][:, 0:T] if m < 4 else BC[:, m - 4, 0:T]
                            dve.wait_ge(*s_ctanh.at(l, g, m))
                            V_.scalar_tensor_tensor(o, th[m % 2][:, 0:T], 1.0, o, ALU.add, ALU.mult).then_inc(s_silu.sem, 1)
                    dve.wait_ge(*s_silu.at(l, g, 5))
                    beside.point("conv", 5)
                    for q in range(2):
                        ins = V_.tensor_copy(Cz[64 * q:64 * q + 64, q, 0:T], BC[64 * q:64 * q + 64, 1, 0:T])
                    chain(ins)
                    dve.wait_ge(*free["pa"].at(l, g, 2 * nb - 1))
                    dt, a, e = (dtt[:, k, 0:nb, :] for k in range(3))
                    bias = par_(l, "dtb", 0, 16).unsqueeze(1).broadcast_to([P, nb, 16])
                    chain(V_.tensor_tensor(dt, tokA[:, 0:nb, OFF_Z:TOK], bias, ALU.add))
                    chain(V_.tensor_scalar(e, dt, -1.0, None, ALU.mult))
                    V_.tensor_tensor(e, e, dt, ALU.max).then_inc(s_dtv.sem, 1)
                    dve.wait_ge(*s_dte.at(l, g))
                    chain(V_.scalar_tensor_tensor(dt, dt, 0.0, e, ALU.max, ALU.add))
                    V_.scalar_tensor_tensor(a, dt, -1.0, aneg[:].unsqueeze(1).broadcast_to([P, nb, 16]), ALU.mult,
                                            ALU.mult).then_inc(s_a.sem, 1)
                    for b in range(nb):
                        t = tile_of("cb", l, g, b)
                        for d in range(2):
                            m = C[:, C_LI if d else C_UI, :].unsqueeze(1).broadcast_to([P, 2, P])
                            ins = V_.tensor_tensor(gm[:, b, d], t[:, 0:2 * P].rearrange("p (g m) -> p g m", g=2), m, ALU.mult)
                        ins.then_inc(free["cb"].sem, 1)
                    dve.wait_ge(*free["pg"].at(l, g, 3))
                    for j in range(2):
                        ins = V_.scalar_tensor_tensor(hcv[:, j, 15:15 + T], cacc[:, j, 0:T], 1.0, hcv[:, j, 15:15 + T], ALU.add, ALU.mult)
                    chain(ins)
                    for k in range(CMK):
                        for j in range(2):
                            w = par_(l, "dw", j * CMK + k)
                            if k == 0:
                                ins = V_.tensor_scalar(cacc[:, j, 0:T], hcv[:, j, 0:T], w, par_(l, "db", j), ALU.mult, ALU.add)
                            else:
                                ins = V_.scalar_tensor_tensor(cacc[:, j, 0:T], hcv[:, j, k:k + T], w, cacc[:, j, 0:T], ALU.mult, ALU.add)
                        if k < CMK - 1:
                            chain(ins)
                            beside.point("taps", k)
                    ins.then_inc(s_glu.sem, 1)
                    for b in range(nb):
                        t = tile_of("ct", l, g, b)
                        chain(V_.bn_stats(bn[:, b, 0:6], t[:, 0:256]))
                        chain(V_.bn_aggr(bn[:, b, 6:8], bn[:, b, 0:6]))
                        rsqrt(st[:, 40 + b:41 + b], bn[:, b, 7:8], 1.0)
                        if b >= 2:
                            dve.wait_ge(*full["cT"].at(l, g, b - 2))
                        chain(V_.tensor_scalar(ctok[b % 2], t[:, 0:256], bn[:, b, 6:7], st[:, 40 + b:41 + b], ALU.subtract, ALU.mult))
                        V_.tensor_copy(nw[:, 2, 0:1], nw[:, 0, 0:1]).then_inc(s_ctok.sem, 1)
                        V_.tensor_copy(nw[:, 2, 1:2], nw[:, 0, 0:1]).then_inc(free["ct"].sem, 1)
                        for m in ((b - 1,) if b < nb - 1 else (b - 1, b)):
                            if m < 0:
                                continue
                            t = tile_of("cT", l, g, m)
                            v = vtmp[m % 2]
                            for j in range(2):
                                ins = V_.tensor_scalar(v[:, j, :], t[:, j * P:(j + 1) * P], par_(l, "lg", j), par_(l, "lb", j), ALU.mult, ALU.add)
                            ins.then_inc(s_carg.sem, 1)
                            dve.wait_ge(*s_cmt.at(l, g, m))
                            V_.scalar_tensor_tensor(hT[:, 6:8, m * P:(m + 1) * P], th[m % 2][:, 0:256].rearrange("p (j m) -> p j m", j=2), 1.0,
                                                    v, ALU.add, ALU.mult).then_inc(free["cT"].sem, 1)
                    beside.point("cT", nb - 1)
                    dve.wait_ge(*full["ct"].at(l, g, nb - 1))
                    V_.memset(Sbd[:], 0.0).then_inc(s_szero.sem, 1)
                    dve.wait_ge(*free["xt"].at(l, g, 4))
                    dskip = par_(l, "sd", 0, 8).unsqueeze(2).broadcast_to([P, SH, SP_])

                    def heads(x):
                        return x.rearrange("p (h m) -> p h m", h=SH)

                    dve.wait_ge(*free["cT"].at(l, g, nb - 1))
                    for b in range(nb):
                        ins = V_.tensor_tensor(heads(yacc[:, b]), heads(xtok[:, b, 0:512]), dskip, ALU.mult)
                    chain(ins)
                    dve.wait_ge(*free["cs"].at(l, g, nb - 1))
                    steps = ssd_steps(g)

                    def decay_rows(i):
                        d, b = steps[i]
                        if i >= 2:
                            dve.wait_ge(*full["y"].at(l, g, i - 2))
                        V_.tensor_tensor(Em[i % 2], C[:, C_LI if d else C_UI, :].unsqueeze(1).broadcast_to([P, SH, P]),
                                         dtt[:, 1, b, 8 * d:8 * d + 8].unsqueeze(2).broadcast_to([P, SH, P]), ALU.mult).then_inc(s_arow.sem, 1)

                    decay_rows(0)
                    for i, (d, b) in enumerate(steps):
                        if i + 1 < len(steps):
                            decay_rows(i + 1)
                        if i:
                            dve.wait_ge(*full["st"].at(l, g, i - 1))
                        chain(V_.tensor_tensor(heads(xdt), heads(xtok[:, b, 0:512]),
                                               dtt[:, 0, b, 8 * d:8 * d + 8].unsqueeze(2).broadcast_to([P, SH, SP_]), ALU.mult))
                        V_.tensor_tensor(heads(xdec), heads(xdt),
                                         ex[:, b, 16 + 8 * d:24 + 8 * d].unsqueeze(2).broadcast_to([P, SH, SP_]), ALU.mult).then_inc(s_xdt.sem, 1)
                        dve.wait_ge(*free["dd"].at(l, g, 2 * i + 1))
                        e4 = Em[i % 2].rearrange("p (g h) m -> p g h m", g=2)
                        V_.tensor_tensor(e4, e4, gm[:, b, d].unsqueeze(2).broadcast_to([P, 2, 4, P]), ALU.mult).then_inc(s_em.sem, 1)
                        t = tile_of("yo", l, g, i)
                        chain(V_.tensor_tensor(heads(ytmp), heads(t), ex[:, b, 8 * d:8 * d + 8].unsqueeze(2).broadcast_to([P, SH, SP_]), ALU.mult))
                        V_.tensor_tensor(yacc[:, b], yacc[:, b], ytmp, ALU.add).then_inc(free["yo"].sem, 1)
                        dve.wait_ge(*free["yo"].at(l, g, i))
                        t = tile_of("y", l, g, i)
                        V_.tensor_tensor(yacc[:, b], yacc[:, b], t, ALU.add).then_inc(free["y"].sem, 1)
                        t = tile_of("st", l, g, i)
                        for q in range(2):
                            s4 = Sbd[64 * q:64 * q + 64, d, 256 * q:256 * q + 256].rearrange("p (h m) -> p h m", h=4)
                            tot = ex[64 * q:64 * q + 64, b, 32 + 8 * d + 4 * q:36 + 8 * d + 4 * q].unsqueeze(2).broadcast_to([64, 4, SP_])
                            ins = V_.tensor_tensor(s4, s4, tot, ALU.mult)
                        chain(ins)
                        for q in range(2):
                            s2 = Sbd[64 * q:64 * q + 64, d, 256 * q:256 * q + 256]
                            ins = V_.tensor_tensor(s2, s2, t[64 * q:64 * q + 64, 256 * q:256 * q + 256], ALU.add)
                            if q == 0:
                                continue
                            chain(ins)
                        V_.tensor_copy(nw[:, 2, 2:3], nw[:, 0, 0:1]).then_inc(free["st"].sem, 1)
                        V_.tensor_copy(nw[:, 2, 3:4], nw[:, 0, 0:1]).then_inc(s_sup.sem, 1)
                        beside.point("st", i)
                    for b in range(nb):
                        V_.scalar_tensor_tensor(yacc[:, b], yacc[:, b], 0.5, zs[:, b], ALU.mult, ALU.mult).then_inc(s_yg.sem, 1)
                    dve.wait_ge(*s_ss["ys"].at(l, g))
                    rsqrt(st[:, 40:40 + nb], st[:, 16:16 + nb], 1.0 / INNER)
                    for b in range(nb):
                        V_.tensor_scalar(yacc[:, b], yacc[:, b], st[:, 40 + b:41 + b], None, ALU.mult).then_inc(s_xn["ys"].sem, 1)
                    beside.point("yT", nb - 1)
                    dve.wait_ge(*s_ss["aq"].at(l, g))
                    sq = st[:, 8:8 + 2 * nb].rearrange("p (b k) -> p b k", k=2)
                    chain(V_.tensor_scalar(sq[:, :, 1], sq[:, :, 1], float(Q_LORA) / KV_LORA, None, ALU.mult))
                    rsqrt(st[:, 32:32 + 2 * nb], st[:, 8:8 + 2 * nb], 1.0 / Q_LORA)
                    dve.wait_ge(*full["yT"].at(l, g, nb - 1))
                    for k in range(2):
                        ins = V_.memset(kp96[k][:, 0:NOPE], 0.0)
                    chain(ins)

                    def rotate(x, b, n):
                        t1, t2 = rtmp[:, 0, 0:n, :], rtmp[:, 1, 0:n, :]
                        V_.tensor_tensor(t1, x, rp[:, b, 0, :].unsqueeze(1).broadcast_to([P, n, ROPE]), ALU.mult)
                        chain(V_.tensor_tensor(t2, x, rp[:, b, 1, :].unsqueeze(1).broadcast_to([P, n, ROPE]), ALU.mult))
                        return t1, t2

                    def halves(x, k):
                        return x.rearrange("p n (a s f) -> p n a s f", a=2, s=2)[:, :, :, k, :]

                    for b in range(nb):
                        V_.tensor_scalar(tokA[:, b, 0:Q_LORA], tokA[:, b, 0:Q_LORA], st[:, 32 + 2 * b:33 + 2 * b], None, ALU.mult)
                        V_.scalar_tensor_tensor(tokA[:, b, Q_LORA:384], tokA[:, b, Q_LORA:384], st[:, 33 + 2 * b:34 + 2 * b],
                                                par_(l, "kvg", 0, 128), ALU.mult, ALU.mult)
                        if b >= 2:
                            dve.wait_ge(*full["at"].at(l, g, b - 2))
                        src, dst = tokA[:, b, 384:416].unsqueeze(1), kp96[b % 2][:, NOPE:QK].unsqueeze(1)
                        if g:
                            t1, t2 = rotate(src, b, 1)
                            V_.tensor_tensor(halves(dst, 0), halves(t1, 0), halves(t2, 1), ALU.subtract)
                            V_.tensor_tensor(halves(dst, 1), halves(t1, 1), halves(t2, 0), ALU.add).then_inc(s_nrm.sem, 1)
                            dve.wait_ge(*s_nrm.at(l, g, b))
                        else:
                            V_.tensor_copy(dst, src).then_inc(s_nrm.sem, 1)
                    for kb in range(KV_BLOCKS[g]):
                        t = tile_of("v", l, g, kb)
                        V_.tensor_copy(V[:, kb, :], t[:, 0:256]).then_inc(free["v"].sem, 1)
                    beside.point("v", KV_BLOCKS[g] - 1)
                    for b in range(nb):
                        if g:
                            dve.wait_ge(*free["q"].at(l, g, b))
                            x = qtok[b % 2].rearrange("p (h m) -> p h m", h=HEADS)[:, :, NOPE:]
                            t1, t2 = rotate(x, b, HEADS)
                            for h in range(HEADS):
                                V_.tensor_tensor(halves(x, 0)[:, h], halves(t1, 0)[:, h], halves(t2, 1)[:, h], ALU.subtract)
                                ins = V_.tensor_tensor(halves(x, 1)[:, h], halves(t1, 1)[:, h], halves(t2, 0)[:, h], ALU.add)
                            ins.then_inc(s_qr.sem, 1)
                            dve.wait_ge(*s_qr.at(l, g, b))
                        for h in range(HEADS + 2):
                            n = b * HEADS + h
                            if h < HEADS:
                                mx = st[:, 52 + 2 * (n % 2):54 + 2 * (n % 2)]
                                if n >= 2:
                                    dve.wait_ge(*free["sc"].at(l, g, (n - 1) * seg - 1))
                                for k, (lo, w_) in enumerate(key_segments(g)):
                                    t = tile_of("sc", l, g, n * seg + k)
                                    ins = V_.tensor_reduce(mx[:, k:k + 1], t[:, 0:w_], AX.X, ALU.max)
                                chain(ins)
                                if seg == 2:
                                    chain(V_.tensor_tensor(mx[:, 0:1], mx[:, 0:1], mx[:, 1:2], ALU.max))
                                V_.tensor_scalar(st[:, 56 + n % 2:57 + n % 2], mx[:, 0:1], -MLA_SCALE, None, ALU.mult).then_inc(s_mx.sem, 1)
                            if 1 <= h <= HEADS:
                                m = n - 1
                                if m >= 2:
                                    dve.wait_ge(*full["o"].at(l, g, m - 2))
                                for k, (lo, w_) in enumerate(key_segments(g)):
                                    t = tile_of("pT", l, g, m * seg + k)
                                    V_.tensor_copy(PT[m % 2].rearrange("p c m -> p (c m)")[:, lo:lo + w_], t[:, 0:w_]).then_inc(free["pT"].sem, 1)
                            if h >= 2:
                                m = n - 2
                                sm = st[:, 48 + 2 * (m % 2):50 + 2 * (m % 2)]
                                ri = st[:, 58 + m % 2:59 + m % 2]
                                dve.wait_ge(*free["sc"].at(l, g, m * seg + seg - 1))
                                if seg == 2:
                                    chain(V_.tensor_tensor(sm[:, 0:1], sm[:, 0:1], sm[:, 1:2], ALU.add))
                                chain(V_.reciprocal(ri, sm[:, 0:1]))
                                if b >= 2 and h == 2:
                                    dve.wait_ge(*full["aT"].at(l, g, b - 2))
                                t = tile_of("o", l, g, m)
                                ins = V_.tensor_scalar(attn[b % 2][:, (h - 2) * VH:(h - 1) * VH], t[:, 0:VH], ri, None, ALU.mult)
                                ins.then_inc(free["o"].sem, 1)
                            beside.point("head", b * (HEADS + 2) + h)
                        dve.wait_ge(*free["o"].at(l, g, b * HEADS + 3))
                        V_.tensor_copy(nw[:, 2, 4:5], nw[:, 0, 0:1]).then_inc(s_attn.sem, 1)
                    for i in range(OUT_UNITS * nb):
                        u, b = i // nb, i % nb
                        t = tile_of("wo", l, g, i)
                        x = X[:, FIRST_BLOCK[g] + b, u * WU:(u + 1) * WU]
                        chain(V_.tensor_tensor(otmp[i % 2], t[:, 0:WU], G[:, 0, g, u * WU:(u + 1) * WU], ALU.mult))
                        V_.tensor_tensor(x, x, otmp[i % 2], ALU.add).then_inc(free["wo"].sem, 1)
                        beside.point("wo", i)
                    norm_cols("n2", l, g, 2, 3)
                    beside.point("n2", 2 * nb - 1)
                    for i in range(16):
                        beside.point("pq", i)

                    def choose(b):
                        lo, hi = slice(0, 8), slice(8, 16)

                        def best(dst, at_, src, rows):
                            for r in range(rows):
                                ins = V_.max(dst[:, r, at_], src(r))
                            chain(ins)

                        def where(dst, val, at_, src, rows):
                            for r in range(rows):
                                ins = V_.max_index(dst[:, r, at_], val[:, r, at_], src(r))
                            chain(ins)

                        def strike(val, src, rows):
                            for r in range(rows):
                                ins = V_.match_replace(src(r), val[:, r, lo], src(r), -3.0e38)
                            chain(ins)

                        key = lambda r: scs[:, r, :]
                        pair = lambda r: cand[:, r].rearrange("p i j -> p (i j)")
                        t4 = tv[:].rearrange("p (h s) k -> p h s k", s=2)
                        f4 = tif[:].rearrange("p (h s) k -> p h s k", s=2)
                        full4 = [P, PH, TOPK, TOPK]

                        def pairs():
                            chain(V_.tensor_copy(tif, ti))
                            chain(V_.tensor_tensor(cand, t4[:, :, 0, :].unsqueeze(3).broadcast_to(full4),
                                                   t4[:, :, 1, :].unsqueeze(2).broadcast_to(full4), ALU.add))

                        def split():
                            V_.tensor_scalar(bi[:, 0], bj, 4, None, ALU.logical_shift_right)
                            chain(V_.tensor_scalar(bi[:, 1], bj, 15, None, ALU.bitwise_and))
                            chain(V_.tensor_copy(bif, bi))

                        def match(s):
                            chain(V_.tensor_tensor(cand, C[:, C_IOTA, 0:TOPK].unsqueeze(1).unsqueeze(1).broadcast_to(full4),
                                                   bif[:, s].unsqueeze(3).broadcast_to(full4), ALU.is_equal))

                        def look_up(s):
                            chain(V_.tensor_tensor(cand, cand, f4[:, :, s, :].unsqueeze(2).broadcast_to(full4), ALU.mult))
                            chain(V_.tensor_reduce(pick[:, s], cand, AX.X, ALU.add))

                        def expert():
                            ix = idxs[:, blk(l, g, b) % 2, :].rearrange("p (h k) -> p h k", h=PH)
                            chain(V_.tensor_scalar(pick[:, 0], pick[:, 0], float(NK), float(l * NEXP), ALU.mult, ALU.add))
                            if blk(l, g, b) >= 2:
                                dve.wait_ge(s_gst, (blk(l, g, b) - 1) * SLOTS)
                            V_.tensor_tensor(ix, pick[:, 0], pick[:, 1], ALU.add).then_inc(s_idx.sem, 1)
                            chain(V_.tensor_copy(gsum[:, 0], bv[:, :, 0]))
                            V_.tensor_tensor(bv, bv, gsum[:, 0].unsqueeze(2).broadcast_to([P, PH, TOPK]), ALU.subtract).then_inc(s_bsub.sem, 1)

                        def start():
                            dve.wait_ge(*free["ps"].at(l, g, 4 * b + 3))
                            best(tv, lo, key, 16)

                        return [start, lambda: where(ti, tv, lo, key, 16), lambda: strike(tv, key, 16),
                                lambda: best(tv, hi, key, 16), lambda: where(ti, tv, hi, key, 16),
                                lambda: (pairs(), best(bv, lo, pair, PH)),
                                lambda: (where(bj, bv, lo, pair, PH), strike(bv, pair, PH)),
                                lambda: (best(bv, hi, pair, PH), where(bj, bv, hi, pair, PH)),
                                lambda: (split(), match(0)), lambda: look_up(0), lambda: match(1),
                                lambda: (look_up(1), expert())]

                    def gates(b):
                        dve.wait_ge(*s_bexp.at(l, g, b))
                        chain(V_.tensor_reduce(gsum[:, 0], bv, AX.X, ALU.add))
                        chain(V_.reciprocal(gsum[:, 1], gsum[:, 0]))
                        V_.tensor_tensor(gat[:, blk(l, g, b) % 2, :].rearrange("p (h k) -> p h k", h=PH), bv,
                                         gsum[:, 1].unsqueeze(2).broadcast_to([P, PH, TOPK]), ALU.mult).then_inc(s_gate.sem, 1)
                        dve.wait_ge(*s_gate.at(l, g, b))

                    dve.wait_ge(*free["pq"].at(l, g, 15))
                    for step in choose(0):
                        step()
                    gates(0)
                    if g == 0:
                        dve.wait_ge(*free["ht"].at(l, 0, 1))
                        beside.start(blk(l, 0, 0))
                        continue
                    beside.rest()
                    for b in range(nb):
                        n = blk(l, g, b)
                        dve.wait_ge(*free["ht"].at(l, g, 2 * b + 1))

                        def rounds(lo, hi):
                            with dve.Fori(lo, hi) as r:
                                for j in range(RING):
                                    dot(n, r, j)
                                    weigh(n, *((r, j - 1) if j else (r - 1, RING - 1)))

                        for j in range(RING):
                            dot(n, 0, j)
                            if j:
                                weigh(n, 0, j - 1)
                        if b + 1 < nb:
                            steps = choose(b + 1)
                            per = (ROUNDS - 1) // len(steps)
                            for k, step in enumerate(steps):
                                rounds(1 + k * per, 1 + (k + 1) * per)
                                step()
                            if 1 + len(steps) * per < ROUNDS:
                                rounds(1 + len(steps) * per, ROUNDS)
                        else:
                            rounds(1, ROUNDS)
                        for j in range(TAIL):
                            dot(n, ROUNDS, j)
                            weigh(n, *((ROUNDS, j - 1) if j else (ROUNDS - 1, RING - 1)))
                        weigh(n, *((ROUNDS, TAIL - 1) if TAIL else (ROUNDS - 1, RING - 1)))
                        if b + 1 < nb:
                            gates(b + 1)
                        add_peer(n)
            dve.wait_ge(s_nfs, 1)
            rsqrt(st[:, 24:24 + NBLK], st[:, 0:NBLK], 1.0 / D)
            for n in range(NBLK):
                V_.scalar_tensor_tensor(X[:, n, :], X[:, n, :], st[:, 24 + n:25 + n], at(2 * D, D), ALU.mult, ALU.mult).then_inc(s_fin, 1)


def kernel(**t):
    import numpy as np
    import concourse.bacc as bacc
    from concourse import mybir as mb
    from concourse.bass_utils import run_bass_kernel_spmd as run

    a = {k: np.asarray(v) for k, v in t.items()}
    f = np.float32

    def cols(x, chunks):
        return x.reshape(L, chunks, P).transpose(0, 2, 1)

    par = np.concatenate([
        cols(a["norm1_g"], 8), cols(a["norm2_g"], 8), cols(a["q_norm_g"], 2),
        a["ssd_conv_w"].reshape(L, SCONV, XCH, P).transpose(0, 3, 2, 1).reshape(L, P, XCH * SCONV), cols(a["ssd_conv_b"], 6),
        cols(a["ssd_norm_g"], 4), a["cm_dw_w"].reshape(L, CMK, 2, P).transpose(0, 3, 2, 1).reshape(L, P, 2 * CMK),
        cols(a["cm_dw_b"], 2), cols(a["cm_ln_g"], 2), cols(a["cm_ln_b"], 2)], axis=2)
    row = np.concatenate([a["kv_norm_g"], a["ssd_dt_bias"].reshape(L, 16), a["ssd_a_log"].reshape(L, 16), a["ssd_d"]], axis=1)
    k, m = np.meshgrid(np.arange(P), np.arange(P), indexing="ij")
    consts = np.stack([k == m, k <= m, k >= m, k > m, k < m, k >= 0, m]).astype(f)
    inv = (10000.0 ** (-np.arange(8, dtype=f) / f(8))).astype(f)
    tok = np.arange(512)
    ang = np.stack([(tok // 64).astype(f)[:, None] * inv, (tok % 64).astype(f)[:, None] * inv], axis=1)
    spread = np.repeat(ang[:, :, None, :], 2, axis=2).reshape(4, P, ROPE)
    rope = np.stack([np.cos(spread), np.sin(spread)], axis=2).astype(f)
    ins = {
        "x_in": np.concatenate([a["x_prompt"][0], a["x_sample"][0]], axis=0),
        "ckvT_c": a["cache_ckv"][0].transpose(0, 2, 1), "kpeT_c": a["cache_kpe"][0].transpose(0, 2, 1),
        "h0": a["state_ssm"][0].reshape(L, 2, SG, 4, SP_, SN).transpose(0, 1, 2, 5, 3, 4).reshape(L, 2, P, 256),
        "condT": np.stack([a["c_ctx"], a["c"][0]]).reshape(2, DC, P).transpose(2, 1, 0),
        "w_ada": a["w_ada"], "b_ada": a["b_ada"], "w_in": a["w_in"], "w_uq": a["w_uq"], "w_ukv": a["w_ukv"],
        "w_out": a["w_out"], "w_pq": a["peer_wq"],
        "keysT": a["peer_keys"].transpose(0, 3, 1, 2).reshape(L, P, 2 * NK),
        "uv": np.concatenate([a["peer_u"], a["peer_v"]], axis=2).reshape(L * NEXP, 2 * D),
        "par": par, "row": row, "consts": consts, "rope": rope, "final_g": a["final_g"],
    }
    outs = {"y_out": (NBLK * P, D), "ckv_out": (L, P, KV_LORA), "kpe_out": (L, P, ROPE), "ssm_out": (L, 2, P, 256)}
    nc = bacc.Bacc("TRN2", target_bir_lowering=False, num_devices=1)
    arrays, args = {}, {}
    for name, x in ins.items():
        arrays[name] = np.ascontiguousarray(x)
        args[name] = nc.dram_tensor(name, arrays[name].shape, mb.dt.from_np(arrays[name].dtype), kind="ExternalInput").ap()
    for name, shape in outs.items():
        args[name] = nc.dram_tensor(name, shape, mb.dt.float32, kind="ExternalOutput").ap()
    build(nc, **args)
    r = run(nc, [arrays], core_ids=[0]).results[0]
    ssm = r["ssm_out"].reshape(L, 2, SG, SN, 4, SP_).transpose(0, 1, 2, 4, 5, 3).reshape(1, L, 2, SH, SP_, SN)
    y = r["y_out"]
    return (y[None, :P], y[None, P:], r["ckv_out"][None], r["kpe_out"][None], ssm)
```

```python
from contextlib import ExitStack

import numpy as np

import concourse.bass as bass
from concourse import mybir

ALU = mybir.AluOpType
ACT = mybir.ActivationFunctionType
AX = mybir.AxisListType
F32 = mybir.dt.float32
U32 = mybir.dt.uint32
I32 = mybir.dt.int32

P = 128
D = 1024
DC = D // P
L = 2
GROUP_BLOCKS = (1, 4)
FIRST_BLOCK = (0, 1)
NBLK = 5
KV_BLOCKS = (1, 5)
EPS = 1e-6
Q_LORA, KV_LORA, ROPE = 256, 128, 32
HEADS, NOPE, VH = 4, 64, 64
QK = NOPE + ROPE
MLA_SCALE = float(QK) ** -0.5
SH, SP_, SN, SG = 8, 64, 64, 2
INNER = SH * SP_
SCONV = 5
XBC = INNER + 2 * SG * SN
XCH = XBC // P
CM = 256
CMK = 31
IN_DIM = Q_LORA + KV_LORA + ROPE + INNER + XBC + 2 * SH + 2 * CM
OFF_Z = Q_LORA + KV_LORA + ROPE
OFF_X = OFF_Z + INNER
OFF_DT = OFF_X + XBC
OFF_G = OFF_DT + 2 * SH
TOK = OFF_Z + 2 * SH
PH, NK, TOPK = 8, 128, 16
NEXP = NK * NK
SLOTS = PH * TOPK
RING = 5
ROUNDS, TAIL = SLOTS // RING, SLOTS % RING
WU = 256
NW = 3
ARENA = 16392
ADA_UNITS = 6 * D // WU
IN_UNITS, OUT_UNITS, PQ_UNITS = 9, D // WU, 2048 // WU
GROUP_UNITS = IN_UNITS + OUT_UNITS + PQ_UNITS
LAYER_UNITS = ADA_UNITS + 2 * GROUP_UNITS

PAR = {}
_at = 0
for _name, _n in (("n1", 8), ("n2", 8), ("qg", 2), ("cw", 30), ("cb", 6), ("sg", 4), ("dw", 62), ("db", 2),
                  ("lg", 2), ("lb", 2), ("kvg", 128), ("dtb", 16), ("alog", 16), ("sd", 8)):
    PAR[_name] = (_at, _at + _n)
    _at += _n
NPAR = _at
COLS = PAR["kvg"][0]
ROWS = NPAR - COLS
C_ID, C_UI, C_LI, C_LS, C_US, C_ONE, C_IOTA = range(7)


FULL_COUNTS = {
    "mod": (ADA_UNITS, 0), "modT": (16, 0),
    "n1": (2, 8), "pa": (2, 8), "pz": (2, 8), "px": (6, 6), "pg": (4, 4),
    "xt": (5, 5), "ct": (1, 4), "cT": (1, 4),
    "cs": (1, 4), "cb": (1, 4), "dd": (4, 16), "y": (2, 8), "yo": (2, 8), "st": (2, 8), "yT": (1, 4),
    "at": (1, 4), "kn": (4, 8), "v": (1, 5), "q": (1, 4), "qT": (1, 4),
    "sc": (4, 32), "pT": (4, 32), "o": (4, 16), "aT": (1, 4),
    "wo": (4, 16), "n2": (2, 8), "pq": (16, 16), "ps": (4, 16), "ht": (2, 8),
}


def ssd_steps(g):
    nb = GROUP_BLOCKS[g]
    return [(i % 2, i // 2 if i % 2 == 0 else nb - 1 - i // 2) for i in range(2 * nb)]


def attn_steps(g):
    return [(b, h) for b in range(GROUP_BLOCKS[g]) for h in range(HEADS)]


def key_segments(g):
    return [(0, P)] if g == 0 else [(0, P), (P, 512)]


def mod_steps():
    out, turned, waiting = [], 0, None
    for u in range(ADA_UNITS):
        out.append(("mod", u, u))
        if waiting is not None:
            out.append(("modT", turned, waiting))
            turned, waiting = turned + 1, None
        if (u // 4) not in (2, 5):
            waiting = u
    return out


def points(*runs):
    return {(stage, i): rows for stage, instances, rows in runs for i in instances}


BESIDE_SAMPLE = points(("n1", [7], 2), ("pa", range(4), 2), ("pa", range(4, 8), 1), ("px", range(6), 1),
                       ("pg", range(4), 1), ("conv", [5], 4), ("taps", range(4, 30, 5), 2), ("cT", [3], 4), ("st", range(8), 3), ("yT", [3], 3), ("v", [4], 3), 
                       ("head", range(0, 24, 2), 2), ("head", range(1, 24, 2), 1), ("wo", range(16), 1), ("n2", [7], 3), ("pq", range(8), 2))
BESIDE_PROMPT = points(("mod", range(24), 2), ("n1", [1], 3), ("pa", range(2), 2), ("pz", range(2), 2), ("px", range(6), 1),
                       ("pg", range(4), 1), ("conv", [5], 2), ("taps", range(4, 30, 5), 1), ("cT", [0], 2), ("st", range(2), 3),
                       ("yT", [0], 2), ("v", [0], 2), ("head", range(6), 2), ("wo", range(4), 2), ("n2", [1], 3),
                       ("pq", range(16), 1))
HALF = PH // 2
SPLIT = HALF * TOPK // RING
CHOICE = 14


class Beside:
    LAST = SLOTS + 2

    def __init__(self, run):
        self.run, self.n, self.m, self.points, self.choice = run, None, self.LAST + 1, {}, {}

    def start(self, n, at_points, choice=None):
        self.n, self.m, self.points, self.choice = n, 0 if choice is None else -CHOICE, at_points, choice

    def advance(self):
        if self.m >= 0:
            self.run(self.n, self.m)
        elif self.m + CHOICE in self.choice:
            self.choice[self.m + CHOICE]()
        self.m += 1

    def point(self, stage, i):
        for _ in range(self.points.get((stage, i), 0)):
            if self.m <= self.LAST:
                self.advance()

    def rest(self):
        while self.m <= self.LAST:
            self.advance()


def psum_order():
    out = []
    for l in range(L):
        out += [(s, l, 0, i) for s, i, _ in mod_steps()]
        for g in range(2):
            nb = GROUP_BLOCKS[g]
            seg = len(key_segments(g))
            for s in ("n1", "pa", "pz", "px", "pg", "xt"):
                out += [(s, l, g, i) for i in range(FULL_COUNTS[s][g])]
            for b in range(nb):
                out += [("cs", l, g, b), ("cb", l, g, b)]
            out += [("ct", l, g, b) for b in range(nb)]
            out += [("cT", l, g, b) for b in range(nb)]
            for i in range(2 * nb):
                out += [("dd", l, g, 2 * i), ("dd", l, g, 2 * i + 1), ("yo", l, g, i), ("y", l, g, i), ("st", l, g, i)]
            out += [("yT", l, g, b) for b in range(nb)]
            out += [("at", l, g, b) for b in range(nb)]
            out += [("kn", l, g, i) for i in range(HEADS * seg)]
            out += [("v", l, g, i) for i in range(KV_BLOCKS[g])]
            for b in range(nb):
                out += [("q", l, g, b), ("qT", l, g, b)]
                for h in range(HEADS + 2):
                    if h < HEADS:
                        out += [("sc", l, g, (b * HEADS + h) * seg + s) for s in range(seg)]
                    if 1 <= h <= HEADS:
                        out += [("pT", l, g, (b * HEADS + h - 1) * seg + s) for s in range(seg)]
                    if h >= 2:
                        out.append(("o", l, g, b * HEADS + h - 2))
                out.append(("aT", l, g, b))
            out += [("wo", l, g, i) for i in range(OUT_UNITS * nb)]
            out += [("n2", l, g, i) for i in range(2 * nb)]
            out += [("pq", l, g, i) for i in range(8)] + [(s, l, g, i) for s in ("ht", "ps") for i in range(2)]
            out += [("pq", l, g, i) for i in range(8, 16)] + [("ps", l, g, 2), ("ps", l, g, 3)]
            for b in range(1, nb):
                out += [("ht", l, g, 2 * b), ("ht", l, g, 2 * b + 1)]
                out += [("ps", l, g, 4 * b + i) for i in range(4)]
    return out


def build(nc, x_in, ckvT_c, kpeT_c, h0, condT, w_ada, b_ada, w_in, w_uq, w_ukv, w_out, w_pq, keysT, uv, par, row, consts,
          rope, final_g, y_out, ckv_out, kpe_out, ssm_out):
    order = psum_order()
    place = {t: n for n, t in enumerate(order)}
    BANKS = 6
    with ExitStack() as ctx:
        def sb(name, shape, dt=F32):
            return ctx.enter_context(nc.sbuf_tensor(name, shape, dt))

        class Stage:
            def __init__(self, name, n=(1, 1), step=1):
                self.sem = ctx.enter_context(nc.semaphore(name))
                self.n, self.step = n, step

            def at(self, l, g=0, i=0):
                return self.sem, (l * sum(self.n) + (self.n[0] if g else 0) + i + 1) * self.step

        acc = ctx.enter_context(nc.psum_tensor("expert_acc", [P, 2, 512], F32))
        rot = ctx.enter_context(nc.psum_tensor("rotating", [P, BANKS, 512], F32))
        full = {s: Stage(f"{s}_full", n) for s, n in FULL_COUNTS.items()}
        free = {s: Stage(f"{s}_drained", n) for s, n in FULL_COUNTS.items()}

        def tile(s, l, g, i):
            return rot[:, place[(s, l, g, i)] % BANKS, :]

        X = sb("x", [P, NBLK, D])
        hT = sb("hT", [P, DC, 512])
        W = sb("w_ring", [P, NW, DC, WU])
        UV = sb("uv_ring", [P, RING, 2 * D])
        G = sb("gates", [P, 5, D])
        C = sb("const_mats", [P, 7, P])
        rp = sb("rope_tables", [P, 4, 2, ROPE])
        pr = sb("params", [P, L, NPAR])
        wuq = sb("w_uq_s", [P, 2, HEADS * QK])
        wukv = sb("w_ukv_s", [P, HEADS * P])
        keys = sb("keys_s", [P, 2, NK])
        modc = sb("modc", [P, 4, DC, 2])
        sc_c = sb("silu_cond", [P, 2, DC, 2])
        st = sb("stats", [P, 64])
        nw = sb("newton", [P, 3, 8])
        dtt = sb("dt", [P, 3, 4, 16])
        ex = sb("decays", [P, 4, 48])
        aneg = sb("a_neg", [P, 16])
        idxs = sb("expert_index", [P, 2, SLOTS], U32)
        gat = sb("expert_gate", [P, 2, SLOTS])
        stage_ix = sb("index_stage", [P, RING], U32)
        dots = sb("u_dot", [P, RING])
        gel = sb("gelu", [P, RING])
        diag = sb("diag", [P, RING, P])
        bn = sb("conv_norm_stats", [P, 4, 8])
        htok_p = sb("prompt_rows", [P, D])
        arena = sb("arena", [P, ARENA])

        used = [0]

        def at(off, *shape, dt=F32):
            n = int(np.prod(shape))
            used[0] = max(used[0], off + n)
            assert off + n <= ARENA, off + n
            a = arena[:, off:off + n]
            if dt is not F32:
                a = a.bitcast(dt)
            if len(shape) > 1:
                names = " ".join(f"d{i}" for i in range(len(shape)))
                a = a.rearrange(f"p ({names}) -> p {names}", **{f"d{i}": s for i, s in enumerate(shape)})
            return a

        xn = [at(k * D, D) for k in range(2)]
        mrow = [at(2048 + k * WU, WU) for k in range(2)]
        brow = [at(2560 + k * WU, WU) for k in range(2)]
        def mixer_tiles(g):
            if g == 0:
                tokA, zs, xtok, BC, Cz, yacc = at(0, 1, TOK), at(432, 1, INNER), at(944, 1, 640), at(1584, 2, P), at(1840, 2, P), at(2096, 1, INNER)
                xbcT, hcv, cacc = at(2608, XCH, 4 + P), at(3400, 2, 30 + P), at(3716, 2, P)
                tz = [at(3972 + k * WU, WU) for k in range(2)]
                th = [at(4484 + k * 256, 256) for k in range(2)]
                ctok = [at(4996 + k * 256, 256) for k in range(2)]
                ctmp = [at(5508 + k * P, P) for k in range(2)]
                vtmp = [at(5764 + k * 256, 2, P) for k in range(2)]
                Em = [at(6276 + k * 1024, SH, P) for k in range(2)]
                xdt, xdec, gm, Sbd, ytmp = at(8324, INNER), at(8836, INNER), at(9348, 1, 2, 2, P), at(9860, 2, INNER), at(10884, INNER)
                KT, V, ckvT, cqT = at(11396, HEADS, P), at(11908, 1, HEADS * VH), at(13188, P), at(13316, 1, 2, P)
                QT = [at(12164 + k * 512, HEADS, P) for k in range(2)]
                kp96 = [at(13572 + k * QK, QK) for k in range(2)]
                qtok = [at(13764 + k * 384, HEADS * QK) for k in range(2)]
                Pm = [at(14532 + k * P, P) for k in range(2)]
                PT = [at(6276 + k * P, 1, P) for k in range(2)]
                attn = [at(2608 + k * 256, 256) for k in range(2)]
                rtmp = at(3400, 2, 1, ROPE)
                otmp = [at(3716 + k * WU, WU) for k in range(2)]
                junk = at(4484, D)
            else:
                tokA = at(0, 4, TOK)
                zs = at(1728, 4, INNER)
                xtok = at(3776, 4, 640)
                BC = at(6336, 2, 512)
                Cz = at(7360, 2, 512)
                yacc = at(8384, 4, INNER)
                xbcT = at(10432, XCH, 516)
                hcv = at(13528, 2, 542)
                cacc = at(14612, 2, 512)
                tz = [at(8384 + k * WU, WU) for k in range(2)]
                th = [at(8896 + k * 512, 512) for k in range(2)]
                ctok = [at(9920 + k * 256, 256) for k in range(2)]
                ctmp = [at(9920, 512), at(15636, 512)]
                vtmp = [at(10432 + k * 256, 2, P) for k in range(2)]
                Em = [at(12992 + k * 1024, SH, P) for k in range(2)]
                xdt = hT[:, 1, :]
                xdec = at(10432, INNER)
                gm = at(10944, 4, 2, 2, P)
                Sbd = at(15040, 2, INNER)
                ytmp = hT[:, 0, :]
                KT = at(1728, HEADS, 640)
                V = at(4288, 5, HEADS * VH)
                QT = [at(5568 + k * 512, HEADS, P) for k in range(2)]
                ckvT = at(6592, 640)
                cqT = at(7232, 4, 2, P)
                kp96 = [at(8256 + k * QK, QK) for k in range(2)]
                qtok = [at(8448 + k * 384, HEADS * QK) for k in range(2)]
                Pm = [at(9216 + k * 640, 640) for k in range(2)]
                PT = [at(10496 + k * 640, 5, P) for k in range(2)]
                attn = [at(11776 + k * 256, 256) for k in range(2)]
                rtmp = at(12288, 2, HEADS, ROPE)
                otmp = [at(12800 + k * WU, WU) for k in range(2)]
                junk = at(8384, D)
            return (tokA, zs, xtok, BC, Cz, yacc, xbcT, hcv, cacc, tz, th, ctok, ctmp, vtmp, Em, xdt, xdec, gm, Sbd, ytmp, KT, V, QT, ckvT, cqT, kp96, qtok, Pm, PT, attn, rtmp, otmp, junk)

        qT = at(0, 16, 512)
        scs = at(8192, 16, NK)
        cand = at(10240, PH, TOPK, TOPK)
        tv = at(12288, 16, TOPK)
        ti = at(12544, 16, TOPK, dt=U32)
        tif = at(12544, 16, TOPK)
        bv = at(12800, PH, TOPK)
        bj = at(12928, PH, TOPK, dt=U32)
        bi = at(13056, 2, PH, TOPK, dt=U32)
        bif = at(13056, 2, PH, TOPK)
        pick = at(13312, 2, PH, TOPK)
        gsum = at(13568, 2, PH)
        htok = [at(13584, D), at(ARENA - 512 - D, D)]
        psum_out = at(ARENA - 512, 512)

        w_loaded = [ctx.enter_context(nc.semaphore(f"w_loaded{k}")) for k in range(NW)]
        s_const = Stage("consts_loaded", step=16)
        s_x = Stage("x_loaded", step=16)
        s_lw = Stage("layer_weights_loaded", (1, 0), 16 * 3)
        s_brow = [Stage(f"b_ada_row_loaded{k}", (ADA_UNITS // 2, 0), 16) for k in range(2)]
        s_condt = Stage("cond_tanh", (1, 0))
        s_cond = Stage("cond_ready", (1, 0))
        s_modc = Stage("modulation_ready", (1, 0))
        s_cache = Stage("cache_loaded", (0, 1), 16 * 2)
        s_szero = Stage("state_cleared", (1, 1))
        s_state = Stage("state_loaded", (0, 1), 16 * 4)
        s_mout = Stage("mixer_outputs_stored", (1, 0), 16 * 6)
        s_out = Stage("outputs_stored", step=16)
        s_ss = {k: Stage(f"{k}_squares", (1, 1)) for k in ("n1", "n2", "aq", "ys", "nf")}
        s_rs = {k: Stage(f"{k}_rstd", (1, 1)) for k in ("n1", "n2", "nf")}
        s_xn = {k: Stage(f"{k}_scaled", (1, 4)) for k in ("n1", "n2", "ys")}
        s_ztanh = Stage("z_tanh", (2, 8))
        s_cconv = Stage("ssd_conv_done", (6, 6))
        s_ctanh = Stage("ssd_conv_tanh", (6, 6))
        s_silu = Stage("ssd_conv_silu", (6, 6))
        s_glu = Stage("conv_module_done")
        s_ctok = Stage("conv_norm_ready", (1, 4))
        s_carg = Stage("conv_silu_argument", (1, 4))
        s_cmt = Stage("conv_silu_tanh", (1, 4))
        s_dtv = Stage("dt_abs")
        s_dte = Stage("dt_log")
        s_a = Stage("a_ready")
        s_arow = Stage("decay_rows_ready", (2, 8))
        s_em = Stage("decay_mask_ready", (2, 8))
        s_xdt = Stage("xdt_ready", (2, 8))
        s_sup = Stage("state_updated", (2, 8))
        s_yg = Stage("y_gated", (1, 4))
        s_nrm = Stage("q_kv_normed", (1, 4))
        s_qr = Stage("q_roped", (0, 4))
        s_mx = Stage("score_max", (4, 16))
        s_attn = Stage("attn_rows_ready", (1, 4))
        s_bsub = Stage("gate_shifted", (1, 5))
        s_bexp = Stage("gate_exp", (1, 5))
        s_idx = Stage("experts_chosen", (1, 5))
        s_gate = Stage("gates_ready", (1, 5))
        s_pup = Stage("peer_added", (1, 4))
        s_fin = ctx.enter_context(nc.semaphore("final_rows_ready"))
        s_nfs = ctx.enter_context(nc.semaphore("final_scaled"))
        s_fg = Stage("final_g_loaded", step=16)
        s_gst = ctx.enter_context(nc.semaphore("indices_staged"))
        s_gat = [ctx.enter_context(nc.semaphore(f"rows_gathered{j}")) for j in range(RING)]
        s_issue = ctx.enter_context(nc.semaphore("gathers_issued"))
        s_dot = ctx.enter_context(nc.semaphore("u_dotted"))
        s_gel = ctx.enter_context(nc.semaphore("gelu_done"))
        s_dg = ctx.enter_context(nc.semaphore("diag_ready"))
        s_vs = ctx.enter_context(nc.semaphore("v_summed"))
        dve_chain = ctx.enter_context(nc.semaphore("dve_chain"))
        act_chain = ctx.enter_context(nc.semaphore("act_chain"))
        pool_chain = ctx.enter_context(nc.semaphore("pool_chain"))

        class Chain:
            def __init__(self, eng, sem):
                self.eng, self.sem, self.n = eng, sem, 0

            def __call__(self, ins):
                self.n += 1
                ins.then_inc(self.sem, 1)
                self.eng.wait_ge(self.sem, self.n)

        def gate_tile(l, which, g):
            return 3 + l % 2 if (which, g) == (1, 1) else 2 * which + g

        def blk(l, g, b):
            return l * NBLK + FIRST_BLOCK[g] + b

        def uses(j):
            return ROUNDS + (1 if j < TAIL else 0)

        def w_unit(l, g, kind, u):
            n = l * LAYER_UNITS
            if kind == "ada":
                return n + u
            return n + ADA_UNITS + g * GROUP_UNITS + {"in": 0, "out": IN_UNITS, "pq": IN_UNITS + OUT_UNITS}[kind] + u

        def unit_left(n):
            l, u = n // LAYER_UNITS, n % LAYER_UNITS
            if u < ADA_UNITS:
                return full["mod"].at(l, 0, u)
            g, u = (u - ADA_UNITS) // GROUP_UNITS, (u - ADA_UNITS) % GROUP_UNITS
            nb = GROUP_BLOCKS[g]
            if u < 2:
                return full["pa"].at(l, g, u * nb + nb - 1)
            if u < 4:
                return full["pz"].at(l, g, (u - 2) * nb + nb - 1)
            if u < 7:
                return full["px"].at(l, g, 2 * (u - 4) + 1)
            if u < IN_UNITS:
                return full["pg"].at(l, g, 2 * (u - 7) + 1)
            u -= IN_UNITS
            if u < OUT_UNITS:
                return full["wo"].at(l, g, u * nb + nb - 1)
            return full["pq"].at(l, g, 2 * (u - OUT_UNITS) + 1)

        block = ctx.enter_context(nc.Block())

        @block.sync
        def _(sp):
            sp.dma_start(C[:], consts.rearrange("c p m -> p c m")).then_inc(s_const.sem, 16)
            sp.dma_start(rp[:], rope.rearrange("b p c r -> p b c r")).then_inc(s_const.sem, 16)
            sp.dma_start(sc_c[:, 0], condT).then_inc(s_const.sem, 16)
            for l in range(L):
                sp.dma_start(pr[:, l, 0:COLS], par[l]).then_inc(s_const.sem, 16)
                sp.dma_start(pr[:, l, COLS:NPAR], row[l:l + 1, :].broadcast_to([P, ROWS])).then_inc(s_const.sem, 16)
            sp.dma_start(X[:], x_in.rearrange("(b p) d -> p b d", p=P)).then_inc(s_x.sem, 16)

            def load_w(n, src):
                if n >= NW:
                    sp.wait_ge(*unit_left(n - NW))
                for k in range(2):
                    sp.dma_start(W[:, n % NW, 4 * k:4 * k + 4, :],
                                 src[512 * k:512 * k + 512, :].rearrange("(c p) n -> p c n", p=P)).then_inc(w_loaded[n % NW], 16)

            for l in range(L):
                if l:
                    sp.wait_ge(*full["ps"].at(l - 1, 1, 15))
                    sp.wait_ge(*full["q"].at(l - 1, 1, 3))
                sp.dma_start(wuq[:], w_uq[l].rearrange("(c p) n -> p c n", p=P)).then_inc(s_lw.sem, 16)
                sp.dma_start(wukv[:], w_ukv[l]).then_inc(s_lw.sem, 16)
                sp.dma_start(keys[:], keysT[l].rearrange("k (s n) -> k s n", s=2)).then_inc(s_lw.sem, 16)
                for u in range(ADA_UNITS):
                    if u >= 2:
                        sp.wait_ge(*free["mod"].at(l, 0, u - 2))
                    sp.dma_start(brow[u % 2], b_ada[l:l + 1, u * WU:(u + 1) * WU].broadcast_to([P, WU])).then_inc(s_brow[u % 2].sem, 16)
                    load_w(w_unit(l, 0, "ada", u), w_ada[l, :, u * WU:(u + 1) * WU])
                for g in range(2):
                    (tokA, zs, xtok, BC, Cz, yacc, xbcT, hcv, cacc, tz, th, ctok, ctmp, vtmp, Em, xdt, xdec, gm, Sbd, ytmp, KT, V, QT, ckvT, cqT, kp96, qtok, Pm, PT, attn, rtmp, otmp, junk) = mixer_tiles(g)
                    for u in range(IN_UNITS):
                        n = w_unit(l, g, "in", u)
                        if u == 1:
                            sp.wait_ge(*unit_left(n - NW))
                            for lo, at_, width in ((256, 0, OFF_Z - 256), (OFF_DT, OFF_Z - 256, 2 * SH)):
                                sp.dma_start(W[:, n % NW, :, at_:at_ + width],
                                             w_in[l, :, lo:lo + width].rearrange("(c p) n -> p c n", p=P)).then_inc(w_loaded[n % NW], 16)
                            continue
                        lo = 0 if u == 0 else OFF_Z + (u - 2) * WU if u < 4 else OFF_X + (u - 4) * WU if u < 7 else OFF_G + (u - 7) * WU
                        load_w(n, w_in[l, :, lo:lo + WU])
                    if g == 1:
                        sp.wait_ge(*s_szero.at(l, 1))
                        for d in range(2):
                            for q in range(2):
                                sp.dma_start(Sbd[64 * q:64 * q + 64, d, 256 * q:256 * q + 256],
                                               h0[l, d, 64 * q:64 * q + 64, :]).then_inc(s_state.sem, 16)
                        sp.wait_ge(*full["yT"].at(l, 1, 3))
                        sp.wait_ge(*s_xn["ys"].at(l, 1, 3))
                        sp.dma_start(ckvT[:, 0:P], ckvT_c[l]).then_inc(s_cache.sem, 16)
                        sp.dma_start(KT[64:96, :, 0:P], kpeT_c[l].unsqueeze(1).broadcast_to([ROPE, HEADS, P])).then_inc(s_cache.sem, 16)
                    else:
                        for d in range(2):
                            sp.wait_ge(*s_sup.at(l, 0, d))
                            for q in range(2):
                                sp.dma_start(ssm_out[l, d, 64 * q:64 * q + 64, :],
                                               Sbd[64 * q:64 * q + 64, d, 256 * q:256 * q + 256]).then_inc(s_mout.sem, 16)
                        sp.wait_ge(*s_nrm.at(l, 0, 0))
                        sp.dma_start(ckv_out[l], tokA[:, 0, Q_LORA:Q_LORA + KV_LORA]).then_inc(s_mout.sem, 16)
                        sp.dma_start(kpe_out[l], tokA[:, 0, Q_LORA + KV_LORA:OFF_Z]).then_inc(s_mout.sem, 16)
                    for u in range(OUT_UNITS):
                        load_w(w_unit(l, g, "out", u), w_out[l, :, u * WU:(u + 1) * WU])
                    for u in range(PQ_UNITS):
                        load_w(w_unit(l, g, "pq", u), w_pq[l, :, u * WU:(u + 1) * WU])
            sp.wait_ge(*s_pup.at(L - 1, 1, 3))
            sp.dma_start(at(2 * D, D), final_g.rearrange("(a n) -> a n", a=1).broadcast_to([P, D])).then_inc(s_fg.sem, 16)
            for n in range(NBLK):
                sp.wait_ge(s_fin, n + 1)
                sp.dma_start(y_out[n * P:(n + 1) * P, :], X[:, n, :]).then_inc(s_out.sem, 16)
            sp.wait_ge(s_out.sem, NBLK * 16)
            sp.wait_ge(*s_mout.at(L - 1))

        @block.gpsimd
        def _(pool):
            for l in range(L):
                for g in range(2):
                    (tokA, zs, xtok, BC, Cz, yacc, xbcT, hcv, cacc, tz, th, ctok, ctmp, vtmp, Em, xdt, xdec, gm, Sbd, ytmp, KT, V, QT, ckvT, cqT, kp96, qtok, Pm, PT, attn, rtmp, otmp, junk) = mixer_tiles(g)
                    nb = GROUP_BLOCKS[g]
                    for b in range(nb):
                        n = blk(l, g, b)
                        base = n * SLOTS
                        halves_ = g == 1 and b == 0
                        pool.wait_ge(*s_idx.at(l, g, 0 if halves_ else b + g))

                        def fetch(r, j):
                            first = isinstance(r, int) and r == 0
                            prev = base - SLOTS + (uses(j) - 1) * RING + j if first else base + r * RING + j - RING
                            if not first or n:
                                pool.wait_ge(s_vs, prev + 1)
                            pool.tensor_copy(stage_ix[:, j:j + 1], idxs[:, n % 2, bass.ds(r * RING + j, 1)]).then_inc(s_gst, 1)
                            pool.wait_ge(s_gst, base + r * RING + j + 1)
                            pool.sem_inc(s_issue, 1)
                            pool.indirect_dma_start(out=UV[:, j, :], out_offset=None, in_=uv,
                                                    in_offset=bass.IndirectOffsetOnAxis(ap=stage_ix[:, j:j + 1], axis=0)).then_inc(s_gat[j], 16)

                        for j in range(RING):
                            fetch(0, j)
                        if halves_:
                            with pool.Fori(1, SPLIT) as r:
                                for j in range(RING):
                                    fetch(r, j)
                            pool.wait_ge(*s_idx.at(l, g, 1))
                        with pool.Fori(SPLIT if halves_ else 1, ROUNDS) as r:
                            for j in range(RING):
                                fetch(r, j)
                        for j in range(TAIL):
                            fetch(ROUNDS, j)

        @block.tensor
        def _(pe):
            fills = iter(order)

            def fill(s, l, g, i):
                assert next(fills) == (s, l, g, i), (s, l, g, i)
                n = place[(s, l, g, i)]
                if n >= BANKS:
                    old = order[n - BANKS]
                    pe.wait_ge(*free[old[0]].at(*old[1:]))
                return rot[:, n % BANKS, :]

            def weights(l, g, kind, u):
                n = w_unit(l, g, kind, u)
                pe.wait_ge(w_loaded[n % NW], 32 * (n // NW + 1))
                return W[:, n % NW]

            def done(ins, s):
                ins.then_inc(full[s].sem, 1)

            def turn(out, src):
                return pe.transpose(out, src, C[:, C_ID, :])

            def norm_T(s, l, g):
                for b in range(GROUP_BLOCKS[g]):
                    pe.wait_ge(*s_xn[s].at(l, g, b))
                    for half in range(2):
                        t = fill(s, l, g, 2 * b + half)
                        for c in range(4):
                            k = 4 * half + c
                            ins = turn(t[:, c * P:(c + 1) * P], xn[b % 2][:, k * P:(k + 1) * P])
                        done(ins, s)

            def add_v(n, r, j, first=False, last=False):
                pe.wait_ge(s_dg, n * SLOTS + r * RING + j + 1)
                for k in range(2):
                    ins = pe.matmul(acc[:, k, :], diag[:, j, :], UV[:, j, D + 512 * k:D + 512 * k + 512],
                                    start=first, stop=last, skip_group_check=True)
                ins.then_inc(s_vs, 1)

            def add_round(n, r):
                if n and r == 0:
                    pe.wait_ge(s_pup.sem, n)
                for j in range(RING if r < ROUNDS else TAIL):
                    add_v(n, r, j, first=(r == 0 and j == 0), last=(r * RING + j == SLOTS - 1))

            def add_beside(n, m):
                if n and m == 2:
                    pe.wait_ge(s_pup.sem, n)
                if 2 <= m <= SLOTS + 1:
                    add_v(n, *divmod(m - 2, RING), first=(m == 2), last=(m == SLOTS + 1))

            beside = Beside(add_beside)

            pe.wait_ge(s_const.sem, 16 * 7)
            for l in range(L):
                pe.wait_ge(*s_cond.at(l))
                for s, i, u in mod_steps():
                    if s == "mod":
                        w = weights(l, 0, "ada", u)
                        t = fill("mod", l, 0, u)
                        for c in range(DC):
                            ins = pe.matmul(t[:, 0:WU], hT[:, c, 0:P], w[:, c, :], start=(c == 0), stop=(c == DC - 1))
                        done(ins, "mod")
                        beside.point("mod", u)
                    else:
                        pe.wait_ge(*free["mod"].at(l, 0, u))
                        t = fill("modT", l, 0, i)
                        for c in range(2):
                            ins = turn(t[:, c * P:(c + 1) * P], mrow[i % 2][:, c * P:(c + 1) * P])
                        done(ins, "modT")

                for g in range(2):
                    (tokA, zs, xtok, BC, Cz, yacc, xbcT, hcv, cacc, tz, th, ctok, ctmp, vtmp, Em, xdt, xdec, gm, Sbd, ytmp, KT, V, QT, ckvT, cqT, kp96, qtok, Pm, PT, attn, rtmp, otmp, junk) = mixer_tiles(g)
                    nb = GROUP_BLOCKS[g]
                    T = nb * P
                    norm_T("n1", l, g)
                    beside.point("n1", 2 * nb - 1)
                    pe.wait_ge(*free["n1"].at(l, g, 2 * nb - 1))
                    for u in range(4):
                        w = weights(l, g, "in", u)
                        s = "pa" if u < 2 else "pz"
                        width = WU if u != 1 else TOK - 256
                        for b in range(nb):
                            t = fill(s, l, g, (u % 2) * nb + b)
                            for c in range(DC):
                                ins = pe.matmul(t[:, 0:width], hT[:, c, b * P:(b + 1) * P], w[:, c, 0:width],
                                                start=(c == 0), stop=(c == DC - 1))
                            done(ins, s)
                            beside.point(s, (u % 2) * nb + b)
                    for u in range(4, IN_UNITS):
                        w = weights(l, g, "in", u)
                        s, first = ("px", 4) if u < 7 else ("pg", 7)
                        for k in range(2):
                            t = fill(s, l, g, 2 * (u - first) + k)
                            for c in range(DC):
                                ins = pe.matmul(t[:, 0:T], w[:, c, k * P:(k + 1) * P], hT[:, c, 0:T],
                                                start=(c == 0), stop=(c == DC - 1))
                            done(ins, s)
                            beside.point(s, 2 * (u - first) + k)
                    for c in range(5):
                        pe.wait_ge(*s_silu.at(l, g, c))
                        t = fill("xt", l, g, c)
                        src = ctmp[c % 2] if c < 4 else BC[:, 0]
                        for b in range(nb):
                            ins = turn(t[:, b * P:(b + 1) * P], src[:, b * P:(b + 1) * P])
                        done(ins, "xt")
                    beside.point("conv", 5)
                    pe.wait_ge(*s_a.at(l, g))
                    pe.wait_ge(*s_silu.at(l, g, 5))
                    for b in range(nb):
                        t = fill("cs", l, g, b)
                        a = dtt[:, 1, b, :]
                        for m, lo, hi, src in ((C_UI, 0, 8, a[:, 0:8]), (C_LI, 8, 16, a[:, 8:16]), (C_LS, 16, 24, a[:, 0:8]),
                                               (C_US, 24, 32, a[:, 8:16]), (C_ONE, 32, 48, a)):
                            ins = pe.matmul(t[:, lo:hi], C[:, m, :], src, start=True, stop=True)
                        done(ins, "cs")
                        t = fill("cb", l, g, b)
                        done(pe.matmul(t[:, 0:2 * P], BC[:, 0, b * P:(b + 1) * P], Cz[:, :, b * P:(b + 1) * P],
                                       start=True, stop=True), "cb")
                    for k in range(CMK):
                        beside.point("taps", k)
                    pe.wait_ge(*s_glu.at(l, g))
                    for b in range(nb):
                        t = fill("ct", l, g, b)
                        for j in range(2):
                            ins = turn(t[:, j * P:(j + 1) * P], cacc[:, j, b * P:(b + 1) * P])
                        done(ins, "ct")
                    for b in range(nb):
                        pe.wait_ge(*s_ctok.at(l, g, b))
                        t = fill("cT", l, g, b)
                        for j in range(2):
                            ins = turn(t[:, j * P:(j + 1) * P], ctok[b % 2][:, j * P:(j + 1) * P])
                        done(ins, "cT")
                    beside.point("cT", nb - 1)
                    for i, (d, b) in enumerate(ssd_steps(g)):
                        pe.wait_ge(*s_arow.at(l, g, i))
                        for k in range(2):
                            t = fill("dd", l, g, 2 * i + k)
                            done(pe.matmul(t, C[:, C_US if d else C_LS, :], Em[i % 2][:, 4 * k:4 * k + 4, :],
                                           start=True, stop=True), "dd")
                        if i >= 2:
                            pe.wait_ge(*s_sup.at(l, g, i - 2))
                        else:
                            pe.wait_ge(*s_szero.at(l, g))
                            if g == 1:
                                pe.wait_ge(*s_state.at(l, 1))
                        t = fill("yo", l, g, i)
                        done(pe.matmul(t, BC[:, 1, b * P:(b + 1) * P], Sbd[:, d, :], start=True, stop=True), "yo")
                        pe.wait_ge(*s_xdt.at(l, g, i))
                        pe.wait_ge(*s_em.at(l, g, i))
                        t = fill("y", l, g, i)
                        for h in range(SH):
                            ins = pe.matmul(t[:, h * SP_:(h + 1) * SP_], Em[i % 2][:, h, :], xdt[:, h * SP_:(h + 1) * SP_],
                                            start=True, stop=True)
                        done(ins, "y")
                        t = fill("st", l, g, i)
                        done(pe.matmul(t, xtok[:, b, 512:640], xdec, start=True, stop=True), "st")
                        beside.point("st", i)
                    for b in range(nb):
                        pe.wait_ge(*s_xn["ys"].at(l, g, b))
                        t = fill("yT", l, g, b)
                        for j in range(4):
                            ins = turn(t[:, j * P:(j + 1) * P], yacc[:, b, j * P:(j + 1) * P])
                        done(ins, "yT")
                    beside.point("yT", nb - 1)
                    for b in range(nb):
                        pe.wait_ge(*s_nrm.at(l, g, b))
                        t = fill("at", l, g, b)
                        for j in range(3):
                            turn(t[:, j * P:(j + 1) * P], tokA[:, b, j * P:(j + 1) * P])
                        done(turn(t[0:QK, 3 * P:4 * P], kp96[b % 2]), "at")
                    pe.wait_ge(*s_lw.at(l))
                    if g == 1:
                        pe.wait_ge(*s_cache.at(l, 1))
                    pe.wait_ge(*free["at"].at(l, g, nb - 1))
                    segs = key_segments(g)
                    for h in range(HEADS):
                        for k, (lo, w_) in enumerate(segs):
                            t = fill("kn", l, g, h * len(segs) + k)
                            done(pe.matmul(t[0:NOPE, 0:w_], wukv[:, h * P:h * P + NOPE], ckvT[:, lo:lo + w_],
                                           start=True, stop=True), "kn")
                    for kb in range(KV_BLOCKS[g]):
                        t = fill("v", l, g, kb)
                        done(pe.matmul(t[:, 0:HEADS * VH], ckvT[:, kb * P:(kb + 1) * P],
                                       wukv[:].rearrange("p (h c) -> p h c", h=HEADS)[:, :, NOPE:], start=True, stop=True), "v")
                    beside.point("v", KV_BLOCKS[g] - 1)
                    for b in range(nb):
                        t = fill("q", l, g, b)
                        for j in range(2):
                            ins = pe.matmul(t[:, 0:HEADS * QK], cqT[:, b, j, :], wuq[:, j, :], start=(j == 0), stop=(j == 1))
                        done(ins, "q")
                        pe.wait_ge(*(s_qr if g else free["q"]).at(l, g, b))
                        t = fill("qT", l, g, b)
                        for h in range(HEADS):
                            ins = turn(t[0:QK, h * P:(h + 1) * P], qtok[b % 2][:, h * QK:(h + 1) * QK])
                        done(ins, "qT")
                        pe.wait_ge(*free["qT"].at(l, g, b))
                        if b == 0:
                            pe.wait_ge(*free["kn"].at(l, g, HEADS * len(segs) - 1))
                            pe.wait_ge(*free["v"].at(l, g, KV_BLOCKS[g] - 1))
                        for h in range(HEADS + 2):
                            n = b * HEADS + h
                            if h < HEADS:
                                for k, (lo, w_) in enumerate(segs):
                                    t = fill("sc", l, g, n * len(segs) + k)
                                    done(pe.matmul(t[:, 0:w_], QT[b % 2][0:QK, h, :], KT[0:QK, h, lo:lo + w_],
                                                   start=True, stop=True), "sc")
                            if 1 <= h <= HEADS:
                                for k, (lo, w_) in enumerate(segs):
                                    pe.wait_ge(*free["sc"].at(l, g, (n - 1) * len(segs) + k))
                                    t = fill("pT", l, g, (n - 1) * len(segs) + k)
                                    for c in range(w_ // P):
                                        ins = turn(t[:, c * P:(c + 1) * P], Pm[(n - 1) % 2][:, lo + c * P:lo + (c + 1) * P])
                                    done(ins, "pT")
                            if h >= 2:
                                m = n - 2
                                pe.wait_ge(*free["pT"].at(l, g, m * len(segs) + len(segs) - 1))
                                t = fill("o", l, g, m)
                                for c in range(KV_BLOCKS[g]):
                                    ins = pe.matmul(t[:, 0:VH], PT[m % 2][:, c, :], V[:, c, (h - 2) * VH:(h - 1) * VH],
                                                    start=(c == 0), stop=(c == KV_BLOCKS[g] - 1))
                                done(ins, "o")
                            beside.point("head", b * (HEADS + 2) + h)
                        pe.wait_ge(*s_attn.at(l, g, b))
                        t = fill("aT", l, g, b)
                        for j in range(2):
                            ins = turn(t[:, j * P:(j + 1) * P], attn[b % 2][:, j * P:(j + 1) * P])
                        done(ins, "aT")
                    for s in ("aT", "yT", "cT"):
                        pe.wait_ge(*free[s].at(l, g, nb - 1))
                    for u in range(OUT_UNITS):
                        w = weights(l, g, "out", u)
                        for b in range(nb):
                            t = fill("wo", l, g, u * nb + b)
                            for c in range(DC):
                                ins = pe.matmul(t[:, 0:WU], hT[:, c, b * P:(b + 1) * P], w[:, c, :],
                                                start=(c == 0), stop=(c == DC - 1))
                            done(ins, "wo")
                            beside.point("wo", u * nb + b)
                    norm_T("n2", l, g)
                    beside.point("n2", 2 * nb - 1)
                    pe.wait_ge(*free["n2"].at(l, g, 2 * nb - 1))
                    def score_block(b, first=0, last=4):
                        for half in range(0 if first else 2):
                            t = fill("ht", l, g, 2 * b + half)
                            for c in range(4):
                                ins = turn(t[:, c * P:(c + 1) * P], hT[:, 4 * half + c, b * P:(b + 1) * P])
                            done(ins, "ht")
                        for k in range(first, last):
                            t = fill("ps", l, g, 4 * b + k)
                            for m in range(4):
                                ins = pe.matmul(t[:, m * P:(m + 1) * P], qT[:, 4 * k + m, b * P:(b + 1) * P],
                                                keys[:, m % 2, :], start=True, stop=True)
                            done(ins, "ps")

                    for u in range(PQ_UNITS):
                        w = weights(l, g, "pq", u)
                        for k in range(2):
                            t = fill("pq", l, g, 2 * u + k)
                            for c in range(DC):
                                ins = pe.matmul(t[:, 0:T], w[:, c, k * P:(k + 1) * P], hT[:, c, 0:T],
                                                start=(c == 0), stop=(c == DC - 1))
                            done(ins, "pq")
                            beside.point("pq", 2 * u + k)
                        if u == 3:
                            pe.wait_ge(*free["pq"].at(l, g, 7))
                            score_block(0, 0, 2)
                    pe.wait_ge(*free["pq"].at(l, g, 15))
                    score_block(0, 2, 4)
                    beside.rest()
                    if g == 0:
                        beside.start(blk(l, 0, 0), BESIDE_SAMPLE, {})
                        continue
                    for b in range(nb):
                        if b + 1 < nb:
                            score_block(b + 1)
                        n = blk(l, g, b)
                        if b + 1 == nb and l + 1 < L:
                            beside.start(n, BESIDE_PROMPT)
                            continue
                        add_round(n, 0)
                        with pe.Fori(1, ROUNDS) as r:
                            for j in range(RING):
                                add_v(n, r, j)
                        if TAIL:
                            add_round(n, ROUNDS)

        @block.scalar
        def _(act):
            chain = Chain(act, act_chain)

            def tile_of(s, l, g, i):
                act.wait_ge(*full[s].at(l, g, i))
                return tile(s, l, g, i)

            def norm_rows(s, l, g, rows):
                nb = GROUP_BLOCKS[g]
                for b in range(nb):
                    ins = nc.scalar.activation(at(4484, D), rows(b), ACT.Square, accum_out=st[:, b:b + 1])
                    if b == nb - 1:
                        ins.then_inc(s_ss[s].sem, 1)
                    else:
                        chain(ins)
                act.wait_ge(*s_rs[s].at(l, g))
                for b in range(nb):
                    if b >= 2:
                        act.wait_ge(*full[s].at(l, g, 2 * (b - 2) + 1))
                    nc.scalar.activation(xn[b % 2], rows(b), ACT.Copy, scale=st[:, 24 + b:25 + b]).then_inc(s_xn[s].sem, 1)

            def gelu(n, r, j):
                act.wait_ge(s_dot, n * SLOTS + r * RING + j + 1)
                nc.scalar.activation(gel[:, j:j + 1], dots[:, j:j + 1], ACT.Gelu).then_inc(s_gel, 1)

            def gelu_round(n, r):
                for j in range(RING if r < ROUNDS else TAIL):
                    gelu(n, r, j)

            def gelu_beside(n, m):
                if m < SLOTS:
                    gelu(n, *divmod(m, RING))

            beside = Beside(gelu_beside)

            act.wait_ge(s_const.sem, 16 * 7)
            act.wait_ge(s_x.sem, 16)
            for l in range(L):
                nc.scalar.activation(sc_c[:, 1], sc_c[:, 0], ACT.Tanh, scale=0.5).then_inc(s_condt.sem, 1)
                chain(nc.scalar.activation(aneg[:], pr[:, l, slice(*PAR["alog"])], ACT.Exp))
                for u in range(ADA_UNITS):
                    beside.point("mod", u)
                for g in range(2):
                    (tokA, zs, xtok, BC, Cz, yacc, xbcT, hcv, cacc, tz, th, ctok, ctmp, vtmp, Em, xdt, xdec, gm, Sbd, ytmp, KT, V, QT, ckvT, cqT, kp96, qtok, Pm, PT, attn, rtmp, otmp, junk) = mixer_tiles(g)
                    nb = GROUP_BLOCKS[g]
                    T = nb * P
                    seg = len(key_segments(g))
                    if g:
                        if l:
                            act.wait_ge(s_pup.sem, blk(l, 0, 0))
                    elif l:
                        act.wait_ge(*s_gate.at(l - 1, 1, 4))
                    norm_rows("n1", l, g, lambda b: X[:, FIRST_BLOCK[g] + b, :])
                    beside.point("n1", 2 * nb - 1)
                    for i in range(2 * nb):
                        t = tile_of("pa", l, g, i)
                        u, b = i // nb, i % nb
                        w_ = WU if u == 0 else TOK - 256
                        nc.scalar.activation(tokA[:, b, u * WU:u * WU + w_], t[:, 0:w_], ACT.Copy).then_inc(free["pa"].sem, 1)
                        beside.point("pa", i)
                    if g:
                        act.wait_ge(*s_gate.at(l, 0, 0))
                    for i in range(2 * nb):
                        t = tile_of("pz", l, g, i)
                        if i >= 2:
                            act.wait_ge(*free["pz"].at(l, g, i - 2))
                        nc.scalar.activation(tz[i % 2], t[:, 0:WU], ACT.Tanh, scale=0.5).then_inc(s_ztanh.sem, 1)
                        beside.point("pz", i)
                    for i in range(6):
                        t = tile_of("px", l, g, i)
                        nc.scalar.activation(xbcT[:, i, 2:2 + T], t[:, 0:T], ACT.Copy).then_inc(free["px"].sem, 1)
                        beside.point("px", i)
                    for i in range(4):
                        t = tile_of("pg", l, g, i)
                        if i < 2:
                            nc.scalar.activation(hcv[:, i, 15:15 + T], t[:, 0:T], ACT.Copy).then_inc(free["pg"].sem, 1)
                        else:
                            nc.scalar.activation(cacc[:, i - 2, 0:T], t[:, 0:T], ACT.Tanh, scale=0.5).then_inc(free["pg"].sem, 1)
                        beside.point("pg", i)
                    for c in range(7):
                        if c < 6:
                            act.wait_ge(*s_cconv.at(l, g, c))
                            if c >= 2:
                                act.wait_ge(*s_silu.at(l, g, c - 2))
                            nc.scalar.activation(th[c % 2][:, 0:T], ctmp[c % 2][:, 0:T] if c < 4 else BC[:, c - 4, 0:T],
                                                 ACT.Tanh).then_inc(s_ctanh.sem, 1)
                        if 1 <= c <= 5:
                            t = tile_of("xt", l, g, c - 1)
                            nc.scalar.activation(xtok[:, 0:nb, (c - 1) * P:c * P], t[:, 0:T].rearrange("p (b m) -> p b m", b=nb),
                                                 ACT.Copy).then_inc(free["xt"].sem, 1)
                    beside.point("conv", 5)
                    act.wait_ge(*s_dtv.at(l, g))
                    chain(nc.scalar.activation(dtt[:, 2, 0:nb, :], dtt[:, 2, 0:nb, :], ACT.Exp, scale=-1.0))
                    nc.scalar.activation(dtt[:, 2, 0:nb, :], dtt[:, 2, 0:nb, :], ACT.Ln, bias=1.0).then_inc(s_dte.sem, 1)
                    for b in range(nb):
                        t = tile_of("cs", l, g, b)
                        nc.scalar.activation(ex[:, b, :], t[:, 0:48], ACT.Exp).then_inc(free["cs"].sem, 1)
                    for k in range(CMK):
                        beside.point("taps", k)
                    for b in range(nb):
                        act.wait_ge(*s_carg.at(l, g, b))
                        if b >= 2:
                            act.wait_ge(*free["cT"].at(l, g, b - 2))
                        nc.scalar.activation(th[b % 2][:, 0:256], vtmp[b % 2].rearrange("p j m -> p (j m)"), ACT.Tanh).then_inc(s_cmt.sem, 1)
                    beside.point("cT", nb - 1)
                    for i in range(2 * nb):
                        for k in range(2):
                            t = tile_of("dd", l, g, 2 * i + k)
                            if k == 0:
                                act.wait_ge(*full["dd"].at(l, g, 2 * i + 1))
                            nc.scalar.activation(Em[i % 2][:, 4 * k:4 * k + 4, :].rearrange("p h m -> p (h m)"), t,
                                                 ACT.Exp).then_inc(free["dd"].sem, 1)
                        beside.point("st", i)
                    for b in range(nb):
                        act.wait_ge(*s_yg.at(l, g, b))
                        ins = nc.scalar.activation(xdt, yacc[:, b, :], ACT.Square, accum_out=st[:, 16 + b:17 + b])
                        if b == nb - 1:
                            ins.then_inc(s_ss["ys"].sem, 1)
                        else:
                            chain(ins)
                    for b in range(nb):
                        t = tile_of("yT", l, g, b)
                        for j in range(4):
                            k = PAR["sg"][0] + j
                            ins = nc.scalar.activation(hT[:, 2 + j, b * P:(b + 1) * P], t[:, j * P:(j + 1) * P], ACT.Copy,
                                                       scale=pr[:, l, k:k + 1])
                        ins.then_inc(free["yT"].sem, 1)
                    beside.point("yT", nb - 1)
                    for b in range(nb):
                        chain(nc.scalar.activation(xdt[:, 0:256], tokA[:, b, 0:256], ACT.Square, accum_out=st[:, 8 + 2 * b:9 + 2 * b]))
                        ins = nc.scalar.activation(xdt[:, 0:128], tokA[:, b, 256:384], ACT.Square, accum_out=st[:, 9 + 2 * b:10 + 2 * b])
                        if b == nb - 1:
                            ins.then_inc(s_ss["aq"].sem, 1)
                        else:
                            chain(ins)
                    KO = P if g else 0
                    for b in range(nb):
                        t = tile_of("at", l, g, b)
                        for j in range(2):
                            k = PAR["qg"][0] + j
                            nc.scalar.activation(cqT[:, b, j, :], t[:, j * P:(j + 1) * P], ACT.Copy, scale=pr[:, l, k:k + 1])
                        nc.scalar.activation(ckvT[:, KO + b * P:KO + (b + 1) * P], t[:, 2 * P:3 * P], ACT.Copy)
                        for h in range(HEADS):
                            ins = nc.scalar.activation(KT[64:96, h, KO + b * P:KO + (b + 1) * P], t[64:96, 3 * P:4 * P], ACT.Copy)
                        ins.then_inc(free["at"].sem, 1)
                    segs = key_segments(g)
                    for h in range(HEADS):
                        for k, (lo, w_) in enumerate(segs):
                            t = tile_of("kn", l, g, h * seg + k)
                            nc.scalar.activation(KT[0:64, h, lo:lo + w_], t[0:64, 0:w_], ACT.Copy).then_inc(free["kn"].sem, 1)
                    beside.point("v", KV_BLOCKS[g] - 1)
                    for b in range(nb):
                        t = tile_of("q", l, g, b)
                        if b >= 2:
                            act.wait_ge(*full["qT"].at(l, g, b - 2))
                        nc.scalar.activation(qtok[b % 2], t[:, 0:HEADS * QK], ACT.Copy).then_inc(free["q"].sem, 1)
                        t = tile_of("qT", l, g, b)
                        if b >= 2:
                            act.wait_ge(*full["sc"].at(l, g, (b - 1) * HEADS * seg - 1))
                        nc.scalar.activation(QT[b % 2][0:QK].rearrange("p h m -> p (h m)"), t[0:QK, :], ACT.Copy).then_inc(free["qT"].sem, 1)
                        for h in range(HEADS + 2):
                            if h >= HEADS:
                                beside.point("head", b * (HEADS + 2) + h)
                                continue
                            n = b * HEADS + h
                            act.wait_ge(*s_mx.at(l, g, n))
                            if n >= 2:
                                act.wait_ge(*full["pT"].at(l, g, (n - 1) * seg - 1))
                                act.wait_ge(*free["o"].at(l, g, n - 2))
                            for k, (lo, w_) in enumerate(segs):
                                t = tile_of("sc", l, g, n * seg + k)
                                c = 48 + (n % 2) * 2 + k
                                nc.scalar.activation(Pm[n % 2][:, lo:lo + w_], t[:, 0:w_], ACT.Exp, scale=MLA_SCALE,
                                                     bias=st[:, 56 + n % 2:57 + n % 2],
                                                     accum_out=st[:, c:c + 1]).then_inc(free["sc"].sem, 1)
                            beside.point("head", b * (HEADS + 2) + h)
                        t = tile_of("aT", l, g, b)
                        nc.scalar.activation(hT[:, 0:2, b * P:(b + 1) * P], t[:, 0:256].rearrange("p (j m) -> p j m", j=2),
                                             ACT.Copy).then_inc(free["aT"].sem, 1)
                    for i in range(OUT_UNITS * nb):
                        beside.point("wo", i)
                    act.wait_ge(*free["wo"].at(l, g, OUT_UNITS * nb - 1))
                    act.wait_ge(*s_mout.at(l))
                    norm_rows("n2", l, g, lambda b: X[:, FIRST_BLOCK[g] + b, :])
                    beside.point("n2", 2 * nb - 1)
                    act.wait_ge(*free["n2"].at(l, g, 2 * nb - 1))
                    def drain_scores(b, first=0, last=4):
                        for half in range(0 if first else 2):
                            t = tile_of("ht", l, g, 2 * b + half)
                            if b >= 2 and half == 0:
                                act.wait_ge(s_dot, (blk(l, g, b) - 1) * SLOTS)
                            nc.scalar.activation((htok[b % 2] if g else htok_p[:])[:, 512 * half:512 * half + 512], t, ACT.Copy).then_inc(free["ht"].sem, 1)
                        for k in range(first, last):
                            t = tile_of("ps", l, g, 4 * b + k)
                            if b and k == 0:
                                act.wait_ge(*s_idx.at(l, g, b - 1 + g))
                            nc.scalar.activation(scs[:, 4 * k:4 * k + 4, :].rearrange("p s n -> p (s n)"), t, ACT.Copy).then_inc(free["ps"].sem, 1)

                    def gate_exp(i, heads=slice(0, PH), l=l, g=g):
                        act.wait_ge(*s_bsub.at(l, g, i))
                        nc.scalar.activation(bv[:, heads], bv[:, heads], ACT.Exp).then_inc(s_bexp.sem, 1)

                    for i in range(16):
                        t = tile_of("pq", l, g, i)
                        nc.scalar.activation(qT[:, i, 0:T], t[:, 0:T], ACT.Copy).then_inc(free["pq"].sem, 1)
                        beside.point("pq", i)
                        if i == 7:
                            drain_scores(0, 0, 2)
                    drain_scores(0, 2, 4)
                    beside.rest()
                    if g == 0:
                        beside.start(blk(l, 0, 0), BESIDE_SAMPLE, {CHOICE - 2: lambda gate_exp=gate_exp: gate_exp(0)})
                        continue
                    gate_exp(0, slice(0, HALF))
                    for b in range(nb):
                        if 0 < b < nb - 1:
                            drain_scores(b + 1)
                        n = blk(l, g, b)
                        if b + 1 == nb and l + 1 < L:
                            beside.start(n, BESIDE_PROMPT)
                            continue
                        if b == 0:
                            with act.Fori(0, 7) as r:
                                for j in range(RING):
                                    gelu(n, r, j)
                            gate_exp(1, slice(HALF, PH))
                            drain_scores(1)
                        with act.Fori(0 if b else 7, ROUNDS) as r:
                            for j in range(RING):
                                gelu(n, r, j)
                        gelu_round(n, ROUNDS)
                        if b + 1 < nb:
                            gate_exp(b + 2)
            act.wait_ge(s_pup.sem, L * NBLK)
            for n in range(NBLK):
                chain(nc.scalar.activation(at(3 * D, D), X[:, n, :], ACT.Square, accum_out=st[:, n:n + 1]))
            act.wait_ge(s_fg.sem, 16)
            nc.scalar.activation(at(3 * D, 1), st[:, 0:1], ACT.Copy).then_inc(s_nfs, 1)

        @block.vector
        def _(dve):
            chain = Chain(dve, dve_chain)
            V_ = nc.vector

            def tile_of(s, l, g, i):
                dve.wait_ge(*full[s].at(l, g, i))
                return tile(s, l, g, i)

            def par_(l, name, i=0, n=1):
                a = PAR[name][0] + i
                return pr[:, l, a:a + n]

            def rsqrt(out, src, scale):
                k = src.shape[1]
                v, t = nw[:, 0, 0:k], nw[:, 1, 0:k]
                chain(V_.tensor_scalar(v, src, scale, EPS, ALU.mult, ALU.add))
                chain(V_.tensor_scalar(out.bitcast(I32), v.bitcast(I32), -0.5, 1597463007.0, ALU.mult, ALU.add))
                for _ in range(3):
                    chain(V_.tensor_tensor(t, out, out, ALU.mult))
                    chain(V_.tensor_tensor(t, t, v, ALU.mult))
                    chain(V_.tensor_scalar(t, t, -0.5, 1.5, ALU.mult, ALU.add))
                    chain(V_.tensor_tensor(out, out, t, ALU.mult))

            def norm_cols(s, l, g, shift, scale):
                nb = GROUP_BLOCKS[g]
                dve.wait_ge(*s_ss[s].at(l, g))
                rsqrt(st[:, 24:24 + nb], st[:, 0:nb], 1.0 / D)
                V_.tensor_copy(nw[:, 2, 0:1], nw[:, 0, 0:1]).then_inc(s_rs[s].sem, 1)
                for b in range(nb):
                    for half in range(2):
                        t = tile_of(s, l, g, 2 * b + half)
                        for c in range(4):
                            k = 4 * half + c
                            ins = V_.tensor_scalar(hT[:, k, b * P:(b + 1) * P], t[:, c * P:(c + 1) * P],
                                                   modc[:, scale, k, g:g + 1], modc[:, shift, k, g:g + 1], ALU.mult, ALU.add)
                        ins.then_inc(free[s].sem, 1)

            def rows_of(n):
                return htok[(n % NBLK - 1) % 2] if n % NBLK else htok_p[:]

            def dot(n, r, j):
                dve.wait_ge(s_gat[j], (n * uses(j) + r + 1) * 16)
                V_.tensor_tensor_reduce(UV[:, j, 0:D], UV[:, j, 0:D], rows_of(n), 1.0, 0.0, ALU.mult, ALU.add,
                                        dots[:, j:j + 1]).then_inc(s_dot, 1)

            def weigh(n, r, j):
                dve.wait_ge(s_gel, n * SLOTS + r * RING + j + 1)
                V_.tensor_scalar(diag[:, j, :], C[:, C_ID, :], gat[:, n % 2, bass.ds(r * RING + j, 1)], gel[:, j:j + 1],
                                 ALU.mult, ALU.mult).then_inc(s_dg, 1)

            def add_peer(n):
                g = 1 if n % NBLK else 0
                tmp = psum_out if g else htok_p[:, 0:512]
                dve.wait_ge(s_vs, (n + 1) * SLOTS)
                for k in range(2):
                    x = X[:, n % NBLK, 512 * k:512 * k + 512]
                    chain(V_.tensor_tensor(tmp, acc[:, k, :], G[:, gate_tile(n // NBLK, 1, g), 512 * k:512 * k + 512], ALU.mult))
                    ins = V_.tensor_tensor(x, x, tmp, ALU.add)
                    if k == 0:
                        chain(ins)
                ins.then_inc(s_pup.sem, 1)

            def dot_beside(n, m):
                if m < SLOTS:
                    dot(n, *divmod(m, RING))
                if 1 <= m <= SLOTS:
                    weigh(n, *divmod(m - 1, RING))
                if m == SLOTS + 2:
                    add_peer(n)

            beside = Beside(dot_beside)

            dve.wait_ge(s_const.sem, 16 * 7)
            dve.wait_ge(s_x.sem, 16)
            for l in range(L):
                for name in ("cw", "cb", "dw", "lg", "lb"):
                    lo, hi = PAR[name]
                    chain(V_.tensor_scalar(pr[:, l, lo:hi], pr[:, l, lo:hi], 0.5, None, ALU.mult))
            for l in range(L):
                if l:
                    dve.wait_ge(*full["ht"].at(l - 1, 1, 7))
                dve.wait_ge(*s_condt.at(l))
                chain(V_.scalar_tensor_tensor(sc_c[:, 1], sc_c[:, 1], 1.0, sc_c[:, 0], ALU.add, ALU.mult))
                chain(V_.tensor_scalar(sc_c[:, 1], sc_c[:, 1], 0.5, None, ALU.mult))
                for k in range(2):
                    ins = V_.tensor_copy(hT[:, :, 64 * k:64 * k + 64], sc_c[:, 1, :, k:k + 1].broadcast_to([P, DC, 64]))
                ins.then_inc(s_cond.sem, 1)
                which = {0: 0, 1: 1, 3: 2, 4: 3}
                turned = 0
                for s, i, u in mod_steps():
                    if s == "mod":
                        t = tile_of("mod", l, 0, u)
                        dve.wait_ge(*s_brow[u % 2].at(l, 0, u // 2))
                        part, col = u // 4, (u % 4) * WU
                        if part in (2, 5):
                            for k in range(2):
                                for q in range(2):
                                    ins = V_.tensor_tensor(G[64 * q:64 * q + 64, gate_tile(l, part // 3, k), col:col + WU],
                                                           t[64 * k:64 * k + 64, 0:WU], brow[u % 2][64 * k:64 * k + 64, :], ALU.add)
                        else:
                            if turned >= 2:
                                dve.wait_ge(*full["modT"].at(l, 0, turned - 2))
                            ins = V_.tensor_tensor(mrow[turned % 2], t[:, 0:WU], brow[u % 2], ALU.add)
                            turned += 1
                        ins.then_inc(free["mod"].sem, 1)
                        beside.point("mod", u)
                    else:
                        t = tile_of("modT", l, 0, i)
                        k = 2 * (u % 4)
                        V_.tensor_copy(modc[:, which[u // 4], k:k + 2, :],
                                       t[:, 0:2 * P].rearrange("p (k m) -> p k m", k=2)[:, :, 0:P:64]).then_inc(free["modT"].sem, 1)
                dve.wait_ge(*free["modT"].at(l, 0, 15))
                for m, name in ((1, "n1"), (3, "n2")):
                    chain(V_.scalar_tensor_tensor(modc[:, m], modc[:, m], 1.0,
                                                  par_(l, name, 0, 8).unsqueeze(2).broadcast_to([P, DC, 2]), ALU.add, ALU.mult))

                for g in range(2):
                    (tokA, zs, xtok, BC, Cz, yacc, xbcT, hcv, cacc, tz, th, ctok, ctmp, vtmp, Em, xdt, xdec, gm, Sbd, ytmp, KT, V, QT, ckvT, cqT, kp96, qtok, Pm, PT, attn, rtmp, otmp, junk) = mixer_tiles(g)
                    nb = GROUP_BLOCKS[g]
                    T = nb * P
                    seg = len(key_segments(g))
                    norm_cols("n1", l, g, 0, 1)
                    beside.point("n1", 2 * nb - 1)
                    for i in range(2 * nb):
                        beside.point("pa", i)
                    for i in range(2 * nb):
                        u, b = i // nb, i % nb
                        dve.wait_ge(*s_ztanh.at(l, g, i))
                        V_.scalar_tensor_tensor(zs[:, b, u * WU:(u + 1) * WU], tz[i % 2], 1.0, tile("pz", l, g, i)[:, 0:WU],
                                                ALU.add, ALU.mult).then_inc(free["pz"].sem, 1)
                        beside.point("pz", i)
                    V_.memset(xbcT[:, :, 0:2], 0.0)
                    V_.memset(xbcT[:, :, 2 + T:4 + T], 0.0)
                    V_.memset(hcv[:, :, 0:15], 0.0)
                    V_.memset(hcv[:, :, 15 + T:30 + T], 0.0)
                    chain(V_.memset(Cz[:], 0.0))
                    for c in range(7):
                        if c < 6:
                            dve.wait_ge(*free["px"].at(l, g, c))
                            if 2 <= c < 4:
                                dve.wait_ge(*full["xt"].at(l, g, c - 2))
                            o = ctmp[c % 2][:, 0:T] if c < 4 else BC[:, c - 4, 0:T]
                            chain(V_.tensor_scalar(o, xbcT[:, c, 0:T], par_(l, "cw", c * SCONV), par_(l, "cb", c), ALU.mult, ALU.add))
                            for k in range(1, SCONV):
                                ins = V_.scalar_tensor_tensor(o, xbcT[:, c, k:k + T], par_(l, "cw", c * SCONV + k), o, ALU.mult, ALU.add)
                                if k < SCONV - 1:
                                    chain(ins)
                            ins.then_inc(s_cconv.sem, 1)
                        for s, i in {0: [("px", i) for i in range(3)], 1: [("px", i) for i in range(3, 6)] + [("pg", i) for i in range(4)]}.get(c, []):
                            beside.point(s, i)
                        if c >= 1:
                            m = c - 1
                            o = ctmp[m % 2][:, 0:T] if m < 4 else BC[:, m - 4, 0:T]
                            dve.wait_ge(*s_ctanh.at(l, g, m))
                            V_.scalar_tensor_tensor(o, th[m % 2][:, 0:T], 1.0, o, ALU.add, ALU.mult).then_inc(s_silu.sem, 1)
                    dve.wait_ge(*s_silu.at(l, g, 5))
                    beside.point("conv", 5)
                    for q in range(2):
                        ins = V_.tensor_copy(Cz[64 * q:64 * q + 64, q, 0:T], BC[64 * q:64 * q + 64, 1, 0:T])
                    chain(ins)
                    dve.wait_ge(*free["pa"].at(l, g, 2 * nb - 1))
                    dt, a, e = (dtt[:, k, 0:nb, :] for k in range(3))
                    bias = par_(l, "dtb", 0, 16).unsqueeze(1).broadcast_to([P, nb, 16])
                    chain(V_.tensor_tensor(dt, tokA[:, 0:nb, OFF_Z:TOK], bias, ALU.add))
                    chain(V_.tensor_scalar(e, dt, -1.0, None, ALU.mult))
                    V_.tensor_tensor(e, e, dt, ALU.max).then_inc(s_dtv.sem, 1)
                    dve.wait_ge(*s_dte.at(l, g))
                    chain(V_.scalar_tensor_tensor(dt, dt, 0.0, e, ALU.max, ALU.add))
                    V_.scalar_tensor_tensor(a, dt, -1.0, aneg[:].unsqueeze(1).broadcast_to([P, nb, 16]), ALU.mult,
                                            ALU.mult).then_inc(s_a.sem, 1)
                    for b in range(nb):
                        t = tile_of("cb", l, g, b)
                        for d in range(2):
                            m = C[:, C_LI if d else C_UI, :].unsqueeze(1).broadcast_to([P, 2, P])
                            ins = V_.tensor_tensor(gm[:, b, d], t[:, 0:2 * P].rearrange("p (g m) -> p g m", g=2), m, ALU.mult)
                        ins.then_inc(free["cb"].sem, 1)
                    dve.wait_ge(*free["pg"].at(l, g, 3))
                    for j in range(2):
                        ins = V_.scalar_tensor_tensor(hcv[:, j, 15:15 + T], cacc[:, j, 0:T], 1.0, hcv[:, j, 15:15 + T], ALU.add, ALU.mult)
                    chain(ins)
                    for k in range(CMK):
                        for j in range(2):
                            w = par_(l, "dw", j * CMK + k)
                            if k == 0:
                                ins = V_.tensor_scalar(cacc[:, j, 0:T], hcv[:, j, 0:T], w, par_(l, "db", j), ALU.mult, ALU.add)
                            else:
                                ins = V_.scalar_tensor_tensor(cacc[:, j, 0:T], hcv[:, j, k:k + T], w, cacc[:, j, 0:T], ALU.mult, ALU.add)
                        if k < CMK - 1:
                            chain(ins)
                            beside.point("taps", k)
                    ins.then_inc(s_glu.sem, 1)
                    for b in range(nb):
                        t = tile_of("ct", l, g, b)
                        chain(V_.bn_stats(bn[:, b, 0:6], t[:, 0:256]))
                        chain(V_.bn_aggr(bn[:, b, 6:8], bn[:, b, 0:6]))
                        rsqrt(st[:, 40 + b:41 + b], bn[:, b, 7:8], 1.0)
                        if b >= 2:
                            dve.wait_ge(*full["cT"].at(l, g, b - 2))
                        chain(V_.tensor_scalar(ctok[b % 2], t[:, 0:256], bn[:, b, 6:7], st[:, 40 + b:41 + b], ALU.subtract, ALU.mult))
                        V_.tensor_copy(nw[:, 2, 0:1], nw[:, 0, 0:1]).then_inc(s_ctok.sem, 1)
                        V_.tensor_copy(nw[:, 2, 1:2], nw[:, 0, 0:1]).then_inc(free["ct"].sem, 1)
                        for m in ((b - 1,) if b < nb - 1 else (b - 1, b)):
                            if m < 0:
                                continue
                            t = tile_of("cT", l, g, m)
                            v = vtmp[m % 2]
                            for j in range(2):
                                ins = V_.tensor_scalar(v[:, j, :], t[:, j * P:(j + 1) * P], par_(l, "lg", j), par_(l, "lb", j), ALU.mult, ALU.add)
                            ins.then_inc(s_carg.sem, 1)
                            dve.wait_ge(*s_cmt.at(l, g, m))
                            V_.scalar_tensor_tensor(hT[:, 6:8, m * P:(m + 1) * P], th[m % 2][:, 0:256].rearrange("p (j m) -> p j m", j=2), 1.0,
                                                    v, ALU.add, ALU.mult).then_inc(free["cT"].sem, 1)
                    beside.point("cT", nb - 1)
                    dve.wait_ge(*full["ct"].at(l, g, nb - 1))
                    V_.memset(Sbd[:], 0.0).then_inc(s_szero.sem, 1)
                    dve.wait_ge(*free["xt"].at(l, g, 4))
                    dskip = par_(l, "sd", 0, 8).unsqueeze(2).broadcast_to([P, SH, SP_])

                    def heads(x):
                        return x.rearrange("p (h m) -> p h m", h=SH)

                    dve.wait_ge(*free["cT"].at(l, g, nb - 1))
                    for b in range(nb):
                        ins = V_.tensor_tensor(heads(yacc[:, b]), heads(xtok[:, b, 0:512]), dskip, ALU.mult)
                    chain(ins)
                    dve.wait_ge(*free["cs"].at(l, g, nb - 1))
                    steps = ssd_steps(g)

                    def decay_rows(i):
                        d, b = steps[i]
                        if i >= 2:
                            dve.wait_ge(*full["y"].at(l, g, i - 2))
                        V_.tensor_tensor(Em[i % 2], C[:, C_LI if d else C_UI, :].unsqueeze(1).broadcast_to([P, SH, P]),
                                         dtt[:, 1, b, 8 * d:8 * d + 8].unsqueeze(2).broadcast_to([P, SH, P]), ALU.mult).then_inc(s_arow.sem, 1)

                    decay_rows(0)
                    for i, (d, b) in enumerate(steps):
                        if i + 1 < len(steps):
                            decay_rows(i + 1)
                        if i:
                            dve.wait_ge(*full["st"].at(l, g, i - 1))
                        chain(V_.tensor_tensor(heads(xdt), heads(xtok[:, b, 0:512]),
                                               dtt[:, 0, b, 8 * d:8 * d + 8].unsqueeze(2).broadcast_to([P, SH, SP_]), ALU.mult))
                        V_.tensor_tensor(heads(xdec), heads(xdt),
                                         ex[:, b, 16 + 8 * d:24 + 8 * d].unsqueeze(2).broadcast_to([P, SH, SP_]), ALU.mult).then_inc(s_xdt.sem, 1)
                        dve.wait_ge(*free["dd"].at(l, g, 2 * i + 1))
                        e4 = Em[i % 2].rearrange("p (g h) m -> p g h m", g=2)
                        V_.tensor_tensor(e4, e4, gm[:, b, d].unsqueeze(2).broadcast_to([P, 2, 4, P]), ALU.mult).then_inc(s_em.sem, 1)
                        t = tile_of("yo", l, g, i)
                        chain(V_.tensor_tensor(heads(ytmp), heads(t), ex[:, b, 8 * d:8 * d + 8].unsqueeze(2).broadcast_to([P, SH, SP_]), ALU.mult))
                        V_.tensor_tensor(yacc[:, b], yacc[:, b], ytmp, ALU.add).then_inc(free["yo"].sem, 1)
                        dve.wait_ge(*free["yo"].at(l, g, i))
                        t = tile_of("y", l, g, i)
                        V_.tensor_tensor(yacc[:, b], yacc[:, b], t, ALU.add).then_inc(free["y"].sem, 1)
                        t = tile_of("st", l, g, i)
                        for q in range(2):
                            s4 = Sbd[64 * q:64 * q + 64, d, 256 * q:256 * q + 256].rearrange("p (h m) -> p h m", h=4)
                            tot = ex[64 * q:64 * q + 64, b, 32 + 8 * d + 4 * q:36 + 8 * d + 4 * q].unsqueeze(2).broadcast_to([64, 4, SP_])
                            ins = V_.tensor_tensor(s4, s4, tot, ALU.mult)
                        chain(ins)
                        for q in range(2):
                            s2 = Sbd[64 * q:64 * q + 64, d, 256 * q:256 * q + 256]
                            ins = V_.tensor_tensor(s2, s2, t[64 * q:64 * q + 64, 256 * q:256 * q + 256], ALU.add)
                            if q == 0:
                                continue
                            chain(ins)
                        V_.tensor_copy(nw[:, 2, 2:3], nw[:, 0, 0:1]).then_inc(free["st"].sem, 1)
                        V_.tensor_copy(nw[:, 2, 3:4], nw[:, 0, 0:1]).then_inc(s_sup.sem, 1)
                        beside.point("st", i)
                    for b in range(nb):
                        V_.scalar_tensor_tensor(yacc[:, b], yacc[:, b], 0.5, zs[:, b], ALU.mult, ALU.mult).then_inc(s_yg.sem, 1)
                    dve.wait_ge(*s_ss["ys"].at(l, g))
                    rsqrt(st[:, 40:40 + nb], st[:, 16:16 + nb], 1.0 / INNER)
                    for b in range(nb):
                        V_.tensor_scalar(yacc[:, b], yacc[:, b], st[:, 40 + b:41 + b], None, ALU.mult).then_inc(s_xn["ys"].sem, 1)
                    beside.point("yT", nb - 1)
                    dve.wait_ge(*s_ss["aq"].at(l, g))
                    sq = st[:, 8:8 + 2 * nb].rearrange("p (b k) -> p b k", k=2)
                    chain(V_.tensor_scalar(sq[:, :, 1], sq[:, :, 1], float(Q_LORA) / KV_LORA, None, ALU.mult))
                    rsqrt(st[:, 32:32 + 2 * nb], st[:, 8:8 + 2 * nb], 1.0 / Q_LORA)
                    dve.wait_ge(*full["yT"].at(l, g, nb - 1))
                    for k in range(2):
                        ins = V_.memset(kp96[k][:, 0:NOPE], 0.0)
                    chain(ins)

                    def rotate(x, b, n):
                        t1, t2 = rtmp[:, 0, 0:n, :], rtmp[:, 1, 0:n, :]
                        V_.tensor_tensor(t1, x, rp[:, b, 0, :].unsqueeze(1).broadcast_to([P, n, ROPE]), ALU.mult)
                        chain(V_.tensor_tensor(t2, x, rp[:, b, 1, :].unsqueeze(1).broadcast_to([P, n, ROPE]), ALU.mult))
                        return t1, t2

                    def halves(x, k):
                        return x.rearrange("p n (a s f) -> p n a s f", a=2, s=2)[:, :, :, k, :]

                    for b in range(nb):
                        V_.tensor_scalar(tokA[:, b, 0:Q_LORA], tokA[:, b, 0:Q_LORA], st[:, 32 + 2 * b:33 + 2 * b], None, ALU.mult)
                        V_.scalar_tensor_tensor(tokA[:, b, Q_LORA:384], tokA[:, b, Q_LORA:384], st[:, 33 + 2 * b:34 + 2 * b],
                                                par_(l, "kvg", 0, 128), ALU.mult, ALU.mult)
                        if b >= 2:
                            dve.wait_ge(*full["at"].at(l, g, b - 2))
                        src, dst = tokA[:, b, 384:416].unsqueeze(1), kp96[b % 2][:, NOPE:QK].unsqueeze(1)
                        if g:
                            t1, t2 = rotate(src, b, 1)
                            V_.tensor_tensor(halves(dst, 0), halves(t1, 0), halves(t2, 1), ALU.subtract)
                            V_.tensor_tensor(halves(dst, 1), halves(t1, 1), halves(t2, 0), ALU.add).then_inc(s_nrm.sem, 1)
                            dve.wait_ge(*s_nrm.at(l, g, b))
                        else:
                            V_.tensor_copy(dst, src).then_inc(s_nrm.sem, 1)
                    for kb in range(KV_BLOCKS[g]):
                        t = tile_of("v", l, g, kb)
                        V_.tensor_copy(V[:, kb, :], t[:, 0:256]).then_inc(free["v"].sem, 1)
                    beside.point("v", KV_BLOCKS[g] - 1)
                    for b in range(nb):
                        if g:
                            dve.wait_ge(*free["q"].at(l, g, b))
                            x = qtok[b % 2].rearrange("p (h m) -> p h m", h=HEADS)[:, :, NOPE:]
                            t1, t2 = rotate(x, b, HEADS)
                            for h in range(HEADS):
                                V_.tensor_tensor(halves(x, 0)[:, h], halves(t1, 0)[:, h], halves(t2, 1)[:, h], ALU.subtract)
                                ins = V_.tensor_tensor(halves(x, 1)[:, h], halves(t1, 1)[:, h], halves(t2, 0)[:, h], ALU.add)
                            ins.then_inc(s_qr.sem, 1)
                            dve.wait_ge(*s_qr.at(l, g, b))
                        for h in range(HEADS + 2):
                            n = b * HEADS + h
                            if h < HEADS:
                                mx = st[:, 52 + 2 * (n % 2):54 + 2 * (n % 2)]
                                if n >= 2:
                                    dve.wait_ge(*free["sc"].at(l, g, (n - 1) * seg - 1))
                                for k, (lo, w_) in enumerate(key_segments(g)):
                                    t = tile_of("sc", l, g, n * seg + k)
                                    ins = V_.tensor_reduce(mx[:, k:k + 1], t[:, 0:w_], AX.X, ALU.max)
                                chain(ins)
                                if seg == 2:
                                    chain(V_.tensor_tensor(mx[:, 0:1], mx[:, 0:1], mx[:, 1:2], ALU.max))
                                V_.tensor_scalar(st[:, 56 + n % 2:57 + n % 2], mx[:, 0:1], -MLA_SCALE, None, ALU.mult).then_inc(s_mx.sem, 1)
                            if 1 <= h <= HEADS:
                                m = n - 1
                                if m >= 2:
                                    dve.wait_ge(*full["o"].at(l, g, m - 2))
                                for k, (lo, w_) in enumerate(key_segments(g)):
                                    t = tile_of("pT", l, g, m * seg + k)
                                    V_.tensor_copy(PT[m % 2].rearrange("p c m -> p (c m)")[:, lo:lo + w_], t[:, 0:w_]).then_inc(free["pT"].sem, 1)
                            if h >= 2:
                                m = n - 2
                                sm = st[:, 48 + 2 * (m % 2):50 + 2 * (m % 2)]
                                ri = st[:, 58 + m % 2:59 + m % 2]
                                dve.wait_ge(*free["sc"].at(l, g, m * seg + seg - 1))
                                if seg == 2:
                                    chain(V_.tensor_tensor(sm[:, 0:1], sm[:, 0:1], sm[:, 1:2], ALU.add))
                                chain(V_.reciprocal(ri, sm[:, 0:1]))
                                if b >= 2 and h == 2:
                                    dve.wait_ge(*full["aT"].at(l, g, b - 2))
                                t = tile_of("o", l, g, m)
                                ins = V_.tensor_scalar(attn[b % 2][:, (h - 2) * VH:(h - 1) * VH], t[:, 0:VH], ri, None, ALU.mult)
                                ins.then_inc(free["o"].sem, 1)
                            beside.point("head", b * (HEADS + 2) + h)
                        dve.wait_ge(*free["o"].at(l, g, b * HEADS + 3))
                        V_.tensor_copy(nw[:, 2, 4:5], nw[:, 0, 0:1]).then_inc(s_attn.sem, 1)
                    for i in range(OUT_UNITS * nb):
                        u, b = i // nb, i % nb
                        t = tile_of("wo", l, g, i)
                        x = X[:, FIRST_BLOCK[g] + b, u * WU:(u + 1) * WU]
                        chain(V_.tensor_tensor(otmp[i % 2], t[:, 0:WU], G[:, gate_tile(l, 0, g), u * WU:(u + 1) * WU], ALU.mult))
                        V_.tensor_tensor(x, x, otmp[i % 2], ALU.add).then_inc(free["wo"].sem, 1)
                        beside.point("wo", i)
                    norm_cols("n2", l, g, 2, 3)
                    beside.point("n2", 2 * nb - 1)
                    def choose(b, i, h0=0, h1=PH, l=l, g=g):
                        lo, hi = slice(0, 8), slice(8, 16)
                        hs, rows_ = slice(h0, h1), slice(2 * h0, 2 * h1)
                        sides, heads_ = range(2 * h0, 2 * h1), range(h0, h1)
                        cd = cand[:, hs]

                        def best(dst, at_, src, rows):
                            for r in rows:
                                ins = V_.max(dst[:, r, at_], src(r))
                            chain(ins)

                        def where(dst, val, at_, src, rows):
                            for r in rows:
                                ins = V_.max_index(dst[:, r, at_], val[:, r, at_], src(r))
                            chain(ins)

                        def strike(val, src, rows):
                            for r in rows:
                                ins = V_.match_replace(src(r), val[:, r, lo], src(r), -3.0e38)
                            chain(ins)

                        key = lambda r: scs[:, r, :]
                        pair = lambda r: cand[:, r].rearrange("p i j -> p (i j)")
                        t4 = tv[:].rearrange("p (h s) k -> p h s k", s=2)
                        f4 = tif[:].rearrange("p (h s) k -> p h s k", s=2)
                        full4 = [P, h1 - h0, TOPK, TOPK]

                        def pairs():
                            chain(V_.tensor_copy(tif[:, rows_], ti[:, rows_]))
                            chain(V_.tensor_tensor(cd, t4[:, hs, 0, :].unsqueeze(3).broadcast_to(full4),
                                                   t4[:, hs, 1, :].unsqueeze(2).broadcast_to(full4), ALU.add))

                        def split():
                            V_.tensor_scalar(bi[:, 0, hs], bj[:, hs], 4, None, ALU.logical_shift_right)
                            chain(V_.tensor_scalar(bi[:, 1, hs], bj[:, hs], 15, None, ALU.bitwise_and))
                            chain(V_.tensor_copy(bif[:, :, hs], bi[:, :, hs]))

                        def match(s):
                            chain(V_.tensor_tensor(cd, C[:, C_IOTA, 0:TOPK].unsqueeze(1).unsqueeze(1).broadcast_to(full4),
                                                   bif[:, s, hs].unsqueeze(3).broadcast_to(full4), ALU.is_equal))

                        def look_up(s):
                            chain(V_.tensor_tensor(cd, cd, f4[:, hs, s, :].unsqueeze(2).broadcast_to(full4), ALU.mult))
                            chain(V_.tensor_reduce(pick[:, s, hs], cd, AX.X, ALU.add))

                        def expert():
                            ix = idxs[:, blk(l, g, b) % 2, :].rearrange("p (h k) -> p h k", h=PH)
                            chain(V_.tensor_scalar(pick[:, 0, hs], pick[:, 0, hs], float(NK), float(l * NEXP), ALU.mult, ALU.add))
                            if blk(l, g, b) >= 2 and h0 == 0:
                                dve.wait_ge(s_gst, (blk(l, g, b) - 1) * SLOTS)
                            V_.tensor_tensor(ix[:, hs], pick[:, 0, hs], pick[:, 1, hs], ALU.add).then_inc(s_idx.sem, 1)
                            chain(V_.tensor_copy(gsum[:, 0, hs], bv[:, hs, 0]))
                            V_.tensor_tensor(bv[:, hs], bv[:, hs], gsum[:, 0, hs].unsqueeze(2).broadcast_to([P, h1 - h0, TOPK]), ALU.subtract).then_inc(s_bsub.sem, 1)

                        def start():
                            dve.wait_ge(*free["ps"].at(l, g, 4 * b + h1 // 2 - 1))
                            best(tv, lo, key, sides)

                        return [start, lambda: where(ti, tv, lo, key, sides), lambda: strike(tv, key, sides),
                                lambda: best(tv, hi, key, sides), lambda: where(ti, tv, hi, key, sides),
                                lambda: (pairs(), best(bv, lo, pair, heads_)),
                                lambda: (where(bj, bv, lo, pair, heads_), strike(bv, pair, heads_)),
                                lambda: (best(bv, hi, pair, heads_), where(bj, bv, hi, pair, heads_)),
                                lambda: (split(), match(0)), lambda: look_up(0), lambda: match(1),
                                lambda: (look_up(1), expert())]

                    def gates(b, i, h0=0, h1=PH, l=l, g=g):
                        hs = slice(h0, h1)
                        dve.wait_ge(*s_bexp.at(l, g, i))
                        chain(V_.tensor_reduce(gsum[:, 0, hs], bv[:, hs], AX.X, ALU.add))
                        chain(V_.reciprocal(gsum[:, 1, hs], gsum[:, 0, hs]))
                        V_.tensor_tensor(gat[:, blk(l, g, b) % 2, :].rearrange("p (h k) -> p h k", h=PH)[:, hs], bv[:, hs],
                                         gsum[:, 1, hs].unsqueeze(2).broadcast_to([P, h1 - h0, TOPK]), ALU.mult).then_inc(s_gate.sem, 1)
                        dve.wait_ge(*s_gate.at(l, g, i))

                    first_half = choose(0, 0, 0, HALF) if g else []
                    for i in range(16):
                        beside.point("pq", i)
                        if i >= 8:
                            for step in first_half[2 * (i - 8):2 * (i - 7)]:
                                step()
                    dve.wait_ge(*free["pq"].at(l, g, 15))
                    beside.rest()
                    if g == 0:
                        dve.wait_ge(*free["ht"].at(l, 0, 1))
                        beside.start(blk(l, 0, 0), BESIDE_SAMPLE, {
                            **dict(enumerate(choose(0, 0))), CHOICE - 1: lambda gates=gates: gates(0, 0)})
                        continue
                    gates(0, 0, 0, HALF)
                    for b in range(nb):
                        n = blk(l, g, b)
                        dve.wait_ge(*free["ht"].at(l, g, 2 * b + 1))
                        if b + 1 == nb and l + 1 < L:
                            beside.start(n, BESIDE_PROMPT)
                            continue

                        def rounds(lo, hi):
                            with dve.Fori(lo, hi) as r:
                                for j in range(RING):
                                    dot(n, r, j)
                                    weigh(n, *((r, j - 1) if j else (r - 1, RING - 1)))

                        for j in range(RING):
                            dot(n, 0, j)
                            if j:
                                weigh(n, 0, j - 1)
                        begin = 1
                        if b == 0:
                            steps = choose(0, 1, HALF, PH)
                            for k in range(6):
                                rounds(1 + k, 2 + k)
                                steps[2 * k]()
                                steps[2 * k + 1]()
                            rounds(7, 8)
                            gates(0, 1, HALF, PH)
                            begin = 8
                        if b + 1 < nb:
                            steps = choose(b + 1, b + 2)
                            for k, step in enumerate(steps):
                                rounds(begin + k * (ROUNDS - begin) // len(steps), begin + (k + 1) * (ROUNDS - begin) // len(steps))
                                step()
                        else:
                            rounds(begin, ROUNDS)
                        for j in range(TAIL):
                            dot(n, ROUNDS, j)
                            weigh(n, *((ROUNDS, j - 1) if j else (ROUNDS - 1, RING - 1)))
                        weigh(n, *((ROUNDS, TAIL - 1) if TAIL else (ROUNDS - 1, RING - 1)))
                        if b + 1 < nb:
                            gates(b + 1, b + 2)
                        add_peer(n)
            dve.wait_ge(s_nfs, 1)
            rsqrt(st[:, 24:24 + NBLK], st[:, 0:NBLK], 1.0 / D)
            for n in range(NBLK):
                V_.scalar_tensor_tensor(X[:, n, :], X[:, n, :], st[:, 24 + n:25 + n], at(2 * D, D), ALU.mult, ALU.mult).then_inc(s_fin, 1)


def kernel(**t):
    import numpy as np
    import concourse.bacc as bacc
    from concourse import mybir as mb
    from concourse.bass_utils import run_bass_kernel_spmd as run

    a = {k: np.asarray(v) for k, v in t.items()}
    f = np.float32

    def cols(x, chunks):
        return x.reshape(L, chunks, P).transpose(0, 2, 1)

    par = np.concatenate([
        cols(a["norm1_g"], 8), cols(a["norm2_g"], 8), cols(a["q_norm_g"], 2),
        a["ssd_conv_w"].reshape(L, SCONV, XCH, P).transpose(0, 3, 2, 1).reshape(L, P, XCH * SCONV), cols(a["ssd_conv_b"], 6),
        cols(a["ssd_norm_g"], 4), a["cm_dw_w"].reshape(L, CMK, 2, P).transpose(0, 3, 2, 1).reshape(L, P, 2 * CMK),
        cols(a["cm_dw_b"], 2), cols(a["cm_ln_g"], 2), cols(a["cm_ln_b"], 2)], axis=2)
    row = np.concatenate([a["kv_norm_g"], a["ssd_dt_bias"].reshape(L, 16), a["ssd_a_log"].reshape(L, 16), a["ssd_d"]], axis=1)
    k, m = np.meshgrid(np.arange(P), np.arange(P), indexing="ij")
    consts = np.stack([k == m, k <= m, k >= m, k > m, k < m, k >= 0, m]).astype(f)
    inv = (10000.0 ** (-np.arange(8, dtype=f) / f(8))).astype(f)
    tok = np.arange(512)
    ang = np.stack([(tok // 64).astype(f)[:, None] * inv, (tok % 64).astype(f)[:, None] * inv], axis=1)
    spread = np.repeat(ang[:, :, None, :], 2, axis=2).reshape(4, P, ROPE)
    rope = np.stack([np.cos(spread), np.sin(spread)], axis=2).astype(f)
    ins = {
        "x_in": np.concatenate([a["x_prompt"][0], a["x_sample"][0]], axis=0),
        "ckvT_c": a["cache_ckv"][0].transpose(0, 2, 1), "kpeT_c": a["cache_kpe"][0].transpose(0, 2, 1),
        "h0": a["state_ssm"][0].reshape(L, 2, SG, 4, SP_, SN).transpose(0, 1, 2, 5, 3, 4).reshape(L, 2, P, 256),
        "condT": np.stack([a["c_ctx"], a["c"][0]]).reshape(2, DC, P).transpose(2, 1, 0),
        "w_ada": a["w_ada"], "b_ada": a["b_ada"], "w_in": a["w_in"], "w_uq": a["w_uq"], "w_ukv": a["w_ukv"],
        "w_out": a["w_out"], "w_pq": a["peer_wq"],
        "keysT": a["peer_keys"].transpose(0, 3, 1, 2).reshape(L, P, 2 * NK),
        "uv": np.concatenate([a["peer_u"], a["peer_v"]], axis=2).reshape(L * NEXP, 2 * D),
        "par": par, "row": row, "consts": consts, "rope": rope, "final_g": a["final_g"],
    }
    outs = {"y_out": (NBLK * P, D), "ckv_out": (L, P, KV_LORA), "kpe_out": (L, P, ROPE), "ssm_out": (L, 2, P, 256)}
    nc = bacc.Bacc("TRN2", target_bir_lowering=False, num_devices=1)
    arrays, args = {}, {}
    for name, x in ins.items():
        arrays[name] = np.ascontiguousarray(x)
        args[name] = nc.dram_tensor(name, arrays[name].shape, mb.dt.from_np(arrays[name].dtype), kind="ExternalInput").ap()
    for name, shape in outs.items():
        args[name] = nc.dram_tensor(name, shape, mb.dt.float32, kind="ExternalOutput").ap()
    build(nc, **args)
    r = run(nc, [arrays], core_ids=[0]).results[0]
    ssm = r["ssm_out"].reshape(L, 2, SG, SN, 4, SP_).transpose(0, 1, 2, 4, 5, 3).reshape(1, L, 2, SH, SP_, SN)
    y = r["y_out"]
    return (y[None, :P], y[None, P:], r["ckv_out"][None], r["kpe_out"][None], ssm)
```
